# Optimizing a Trainium2 kernel written in Bass

```python
import math
import jax, jax.numpy as jnp
from jax import lax
import numpy as np

D_MODEL = 1024
BATCH = 1
SEQ = 256
DEPTH = 1

N_META = 16
BLOCK = 128
PAD_FRONT = BLOCK - N_META
N_HEADS = 8
QK_NOPE = 64
QK_ROPE = 32
V_DIM = 64
Q_LORA = 256
KV_LORA = 128
ROPE_THETA = 10000.0
ATTN_SCALE = (QK_NOPE + QK_ROPE) ** -0.5
ATTN_WIDTH = N_HEADS * V_DIM
CONV_DIM = 512
CONV_GROUPS = 8
CONV_W = 3
MIX_WIDTH = ATTN_WIDTH + CONV_DIM
IN_COLS = Q_LORA + KV_LORA + QK_ROPE + 3 * CONV_DIM
SPLITS = [Q_LORA, Q_LORA + KV_LORA, Q_LORA + KV_LORA + QK_ROPE,
          Q_LORA + KV_LORA + QK_ROPE + CONV_DIM, Q_LORA + KV_LORA + QK_ROPE + 2 * CONV_DIM]
N_GROUPS = 4
EXPERTS_PER_GROUP = 8
N_EXPERTS = N_GROUPS * EXPERTS_PER_GROUP
TOP_K = 2
D_FF = 256
EPS = 1e-6
NEG_INF = -1e30


def rms_norm(x, g):
    xf = x.astype(jnp.float32)
    y = xf * lax.rsqrt(jnp.mean(xf * xf, axis=-1, keepdims=True) + EPS)
    return (y * g.astype(jnp.float32)).astype(x.dtype)

def rope_angles(pos):
    inv_freq = 1.0 / (ROPE_THETA ** (jnp.arange(0, QK_ROPE, 2, dtype=jnp.float32) / QK_ROPE))
    ang = pos.astype(jnp.float32)[..., None] * inv_freq
    return jnp.cos(ang), jnp.sin(ang)

def apply_rope(x, cos, sin):
    xf = x.astype(jnp.float32)
    x1, x2 = jnp.split(xf, 2, axis=-1)
    return jnp.concatenate([x1 * cos - x2 * sin, x2 * cos + x1 * sin], axis=-1).astype(x.dtype)

def causal_block_attention(q_nope, q_rope, k_nope, k_rope, v):
    bsz, plen = q_nope.shape[0], q_nope.shape[1]
    nb = plen // BLOCK
    qn = q_nope.reshape(bsz, nb, BLOCK, N_HEADS, QK_NOPE).transpose(1, 0, 2, 3, 4)
    qr = q_rope.reshape(bsz, nb, BLOCK, N_HEADS, QK_ROPE).transpose(1, 0, 2, 3, 4)
    starts = jnp.arange(nb, dtype=jnp.int32) * BLOCK
    k_idx = jnp.arange(plen, dtype=jnp.int32)

    def one_block(args):
        qn_b, qr_b, s0 = args
        s = (jnp.einsum('bqhd,bkhd->bhqk', qn_b, k_nope, preferred_element_type=jnp.float32)
             + jnp.einsum('bqhr,bkr->bhqk', qr_b, k_rope, preferred_element_type=jnp.float32)) * ATTN_SCALE
        q_idx = s0 + jnp.arange(BLOCK, dtype=jnp.int32)
        mask = (k_idx[None, :] >= PAD_FRONT) & (k_idx[None, :] <= q_idx[:, None])
        s = jnp.where(mask[None, None], s, NEG_INF)
        p = jax.nn.softmax(s, axis=-1).astype(v.dtype)
        return jnp.einsum('bhqk,bkhd->bqhd', p, v)

    out = lax.map(one_block, (qn, qr, starts))
    return out.transpose(1, 0, 2, 3, 4).reshape(bsz, plen, N_HEADS * V_DIM)

def hybrid_mixer(h, cos, sin, w_in, q_norm, w_uq, kv_norm, w_ukv, conv_w,
                 attn_out_norm, conv_out_norm, w_out):
    bsz = h.shape[0]
    hp = jnp.pad(h, ((0, 0), (PAD_FRONT, 0), (0, 0)))
    plen = hp.shape[1]
    z = hp @ w_in
    c_q, c_kv, k_pe, gate_b, gate_c, x_in = jnp.split(z, SPLITS, axis=-1)

    q = (rms_norm(c_q, q_norm) @ w_uq).reshape(bsz, plen, N_HEADS, QK_NOPE + QK_ROPE)
    q_nope = q[..., :QK_NOPE]
    q_rope = apply_rope(q[..., QK_NOPE:], cos[:, :, None, :], sin[:, :, None, :])
    kv = (rms_norm(c_kv, kv_norm) @ w_ukv).reshape(bsz, plen, N_HEADS, QK_NOPE + V_DIM)
    k_nope, v = kv[..., :QK_NOPE], kv[..., QK_NOPE:]
    k_rope = apply_rope(k_pe, cos, sin)
    attn = causal_block_attention(q_nope, q_rope, k_nope, k_rope, v)

    u = gate_c * x_in
    u_pad = jnp.pad(u, ((0, 0), (CONV_W - 1, 0), (0, 0)))
    y = sum(conv_w[k] * u_pad[:, k:k + plen] for k in range(CONV_W))
    conv = gate_b * y

    merged = jnp.concatenate([rms_norm(attn[:, PAD_FRONT:], attn_out_norm),
                              rms_norm(conv[:, PAD_FRONT:], conv_out_norm)], axis=-1)
    return merged @ w_out

def hier_moe(h, w_group_router, b_group_router, w_expert_router, b_expert_router,
             w_gate, w_up, w_down, w_sh_gate, w_sh_up, w_sh_down):
    bsz, slen, d = h.shape
    t = h.reshape(-1, d)
    g_prob = jax.nn.softmax((t @ w_group_router).astype(jnp.float32) + b_group_router.astype(jnp.float32), axis=-1)
    g_w, g_idx = lax.top_k(g_prob, 1)
    e_logits = ((t @ w_expert_router).astype(jnp.float32) + b_expert_router.astype(jnp.float32))
    e_logits = e_logits.reshape(-1, N_GROUPS, EXPERTS_PER_GROUP)
    e_logits = jnp.take_along_axis(e_logits, g_idx[:, :, None], axis=1)[:, 0]
    e_prob = jax.nn.softmax(e_logits, axis=-1)
    e_w, e_idx = lax.top_k(e_prob, TOP_K)
    e_w = e_w / jnp.sum(e_w, axis=-1, keepdims=True)
    weights = g_w * e_w
    eid = g_idx * EXPERTS_PER_GROUP + e_idx
    combine = jnp.einsum('nk,nke->ne', weights,
                         jax.nn.one_hot(eid, N_EXPERTS, dtype=jnp.float32)).astype(t.dtype)
    a = jnp.einsum('nd,edf->nef', t, w_gate)
    b = jnp.einsum('nd,edf->nef', t, w_up)
    hid = jax.nn.silu(a) * b * combine[:, :, None]
    routed = jnp.einsum('nef,efd->nd', hid, w_down)
    shared = (jax.nn.silu(t @ w_sh_gate) * (t @ w_sh_up)) @ w_sh_down
    return (routed + shared).reshape(bsz, slen, d)

def first_inputs(seed: int = 0) -> dict:
    key = jax.random.key(seed)
    ks = jax.random.split(key, 32)
    f32 = jnp.float32

    def nrm(k, shape, fan_in):
        return jax.random.normal(k, shape, f32) * (fan_in ** -0.5)

    def gain(k, shape):
        return 1.0 + 0.05 * jax.random.normal(k, shape, f32)

    L = DEPTH
    return {
        "x": jax.random.normal(ks[0], (BATCH, SEQ, D_MODEL), f32),
        "positions": jnp.broadcast_to(jnp.arange(SEQ, dtype=jnp.int32), (BATCH, SEQ)),
        "meta_tokens": jax.random.normal(ks[1], (N_META, D_MODEL), f32),
        "pre_mix_norm": gain(ks[2], (L, D_MODEL)),
        "w_in": nrm(ks[3], (L, D_MODEL, IN_COLS), D_MODEL),
        "q_norm": gain(ks[4], (L, Q_LORA)),
        "w_uq": nrm(ks[5], (L, Q_LORA, N_HEADS * (QK_NOPE + QK_ROPE)), Q_LORA),
        "kv_norm": gain(ks[6], (L, KV_LORA)),
        "w_ukv": nrm(ks[7], (L, KV_LORA, N_HEADS * (QK_NOPE + V_DIM)), KV_LORA),
        "conv_w": nrm(ks[8], (L, CONV_W, CONV_DIM), CONV_W),
        "attn_out_norm": gain(ks[9], (L, ATTN_WIDTH)),
        "conv_out_norm": gain(ks[10], (L, CONV_DIM)),
        "w_out": nrm(ks[11], (L, MIX_WIDTH, D_MODEL), MIX_WIDTH),
        "post_mix_norm": gain(ks[12], (L, D_MODEL)),
        "pre_ffn_norm": gain(ks[13], (L, D_MODEL)),
        "w_group_router": nrm(ks[14], (L, D_MODEL, N_GROUPS), D_MODEL),
        "b_group_router": 0.01 * jax.random.normal(ks[15], (L, N_GROUPS), f32),
        "w_expert_router": nrm(ks[16], (L, D_MODEL, N_EXPERTS), D_MODEL),
        "b_expert_router": 0.01 * jax.random.normal(ks[17], (L, N_EXPERTS), f32),
        "w_gate": nrm(ks[18], (L, N_EXPERTS, D_MODEL, D_FF), D_MODEL),
        "w_up": nrm(ks[19], (L, N_EXPERTS, D_MODEL, D_FF), D_MODEL),
        "w_down": nrm(ks[20], (L, N_EXPERTS, D_FF, D_MODEL), D_FF),
        "w_sh_gate": nrm(ks[21], (L, D_MODEL, D_FF), D_MODEL),
        "w_sh_up": nrm(ks[22], (L, D_MODEL, D_FF), D_MODEL),
        "w_sh_down": nrm(ks[23], (L, D_FF, D_MODEL), D_FF),
        "post_ffn_norm": gain(ks[24], (L, D_MODEL)),
    }

def first_block(x, positions, meta_tokens, pre_mix_norm, w_in, q_norm, w_uq, kv_norm, w_ukv, conv_w,
              attn_out_norm, conv_out_norm, w_out, post_mix_norm, pre_ffn_norm,
              w_group_router, b_group_router, w_expert_router, b_expert_router,
              w_gate, w_up, w_down, w_sh_gate, w_sh_up, w_sh_down, post_ffn_norm):
    bsz = x.shape[0]
    meta = jnp.broadcast_to(meta_tokens[None].astype(x.dtype), (bsz, N_META, D_MODEL))
    h = jnp.concatenate([meta, x], axis=1)
    rope_pos = jnp.concatenate([
        jnp.zeros((bsz, PAD_FRONT), jnp.int32),
        jnp.broadcast_to(jnp.arange(N_META, dtype=jnp.int32), (bsz, N_META)),
        positions.astype(jnp.int32) + N_META], axis=1)
    cos, sin = rope_angles(rope_pos)

    for l in range(DEPTH):
        mix = hybrid_mixer(rms_norm(h, pre_mix_norm[l]), cos, sin, w_in[l], q_norm[l], w_uq[l],
                           kv_norm[l], w_ukv[l], conv_w[l], attn_out_norm[l], conv_out_norm[l], w_out[l])
        h = h + rms_norm(mix, post_mix_norm[l])
        ffn = hier_moe(rms_norm(h, pre_ffn_norm[l]), w_group_router[l], b_group_router[l],
                       w_expert_router[l], b_expert_router[l], w_gate[l], w_up[l], w_down[l],
                       w_sh_gate[l], w_sh_up[l], w_sh_down[l])
        h = h + rms_norm(ffn, post_ffn_norm[l])

    return h[:, N_META:]


POOL_WIDTH = 512
POOL_WINDOWS = (2, 4, 8, 16)
N_POOL_GROUPS = len(POOL_WINDOWS)
POOL_GROUP = POOL_WIDTH // N_POOL_GROUPS
N_Q_HEADS = 8
N_KV_HEADS = 2
HEAD_DIM = 64
Q_GROUP = N_Q_HEADS // N_KV_HEADS
Q_WIDTH = N_Q_HEADS * HEAD_DIM
KV_WIDTH = N_KV_HEADS * HEAD_DIM
WINDOW = 128
N_BRANCHES = 2
IN_WIDTH = POOL_WIDTH + Q_WIDTH + 2 * KV_WIDTH + N_BRANCHES * D_MODEL
D_FF_2 = ((8 * D_MODEL + 3 * 256 - 1) // (3 * 256)) * 256


def rms_norm_2(x, gain):
    xf = x.astype(jnp.float32)
    y = xf * lax.rsqrt(jnp.mean(xf * xf, axis=-1, keepdims=True) + EPS)
    return (y * gain.astype(jnp.float32)).astype(x.dtype)

def alibi_slopes():
    h = jnp.arange(1, N_Q_HEADS + 1, dtype=jnp.float32)
    return jnp.exp2(-8.0 * h / N_Q_HEADS)

def multiscale_pool(z, w_group, scale):
    B, S, _ = z.shape
    zf = z.astype(jnp.float32)
    cs = jnp.pad(jnp.cumsum(zf, axis=1), ((0, 0), (1, 0), (0, 0)))
    t = jnp.arange(S)
    outs = []
    for g, w in enumerate(POOL_WINDOWS):
        sl = slice(g * POOL_GROUP, (g + 1) * POOL_GROUP)
        lo = jnp.clip(t - w // 2, 0, S)
        hi = jnp.clip(t + w // 2, 0, S)
        csg = cs[..., sl]
        count = (hi - lo).astype(jnp.float32)[None, :, None]
        mean = (csg[:, hi] - csg[:, lo]) / count
        outs.append(mean - zf[..., sl])
    d = jnp.stack(outs, axis=2).astype(z.dtype)
    y = jnp.einsum("bsgc,gcd->bsgd", d, w_group).reshape(B, S, POOL_WIDTH)
    return y * scale

def band_blocks(t, nb):
    B = t.shape[0]
    t = jnp.pad(t, ((0, 0), (BLOCK, BLOCK), (0, 0), (0, 0)))
    t = t.reshape(B, nb + 2, BLOCK, N_KV_HEADS, HEAD_DIM)
    return jnp.concatenate([t[:, :-2], t[:, 1:-1], t[:, 2:]], axis=2)

def windowed_gqa(q, k, v, sink):
    B, S, _ = q.shape
    nb = S // BLOCK
    qb = (q * (HEAD_DIM ** -0.5)).reshape(B, nb, BLOCK, N_KV_HEADS, Q_GROUP, HEAD_DIM)
    kb = band_blocks(k.reshape(B, S, N_KV_HEADS, HEAD_DIM), nb)
    vb = band_blocks(v.reshape(B, S, N_KV_HEADS, HEAD_DIM), nb)
    scores = jnp.einsum("bnqhgd,bnkhd->bnhgqk", qb, kb).astype(jnp.float32)
    a = jnp.arange(BLOCK)[:, None]
    c = jnp.arange(3 * BLOCK)[None, :]
    absdist = jnp.abs(a - c + BLOCK)
    kpos = (jnp.arange(nb)[:, None] - 1) * BLOCK + jnp.arange(3 * BLOCK)[None, :]
    kvalid = (kpos >= 0) & (kpos < S)
    mask = (absdist <= WINDOW)[None, :, :] & kvalid[:, None, :]
    slopes = alibi_slopes().reshape(N_KV_HEADS, Q_GROUP)[:, :, None, None]
    scores = scores - slopes * absdist.astype(jnp.float32)
    scores = jnp.where(mask[None, :, None, None, :, :], scores, -jnp.inf)
    sink_l = sink.astype(jnp.float32).reshape(N_KV_HEADS, Q_GROUP)[:, :, None, None]
    m = jnp.maximum(jnp.max(scores, axis=-1, keepdims=True), sink_l)
    p = jnp.exp(scores - m)
    denom = jnp.sum(p, axis=-1, keepdims=True) + jnp.exp(sink_l - m)
    p = (p / denom).astype(v.dtype)
    out = jnp.einsum("bnhgqk,bnkhd->bnqhgd", p, vb)
    return out.reshape(B, S, Q_WIDTH)

def second_inputs(seed: int = 0) -> dict:
    key = jax.random.key(seed)
    ks = jax.random.split(key, 16)
    f32 = jnp.float32

    def dense(k, shape, fan_in):
        return jax.random.normal(k, shape, f32) * (fan_in ** -0.5)

    def gain(k, shape):
        return 1.0 + 0.05 * jax.random.normal(k, shape, f32)

    return {
        "x": jax.random.normal(ks[0], (BATCH, SEQ, D_MODEL), f32),
        "norm_mix": gain(ks[1], (DEPTH, D_MODEL)),
        "w_in": dense(ks[2], (DEPTH, D_MODEL, IN_WIDTH), D_MODEL),
        "w_pool_group": dense(ks[3], (DEPTH, N_POOL_GROUPS, POOL_GROUP, POOL_GROUP), POOL_GROUP),
        "pool_scale": gain(ks[4], (DEPTH, POOL_WIDTH)),
        "sink": 0.5 * jax.random.normal(ks[5], (DEPTH, N_Q_HEADS), f32),
        "w_pool_branch": dense(ks[6], (DEPTH, POOL_WIDTH, D_MODEL), POOL_WIDTH),
        "w_attn_branch": dense(ks[7], (DEPTH, Q_WIDTH, D_MODEL), Q_WIDTH),
        "w_out": dense(ks[8], (DEPTH, D_MODEL, D_MODEL), D_MODEL),
        "norm_ffn": gain(ks[9], (DEPTH, D_MODEL)),
        "w_ffn_gate": dense(ks[10], (DEPTH, D_MODEL, D_FF_2), D_MODEL),
        "w_ffn_up": dense(ks[11], (DEPTH, D_MODEL, D_FF_2), D_MODEL),
        "w_ffn_down": dense(ks[12], (DEPTH, D_FF_2, D_MODEL), D_FF_2),
        "norm_final": gain(ks[13], (D_MODEL,)),
    }

def second_block(x, norm_mix, w_in, w_pool_group, pool_scale, sink, w_pool_branch,
              w_attn_branch, w_out, norm_ffn, w_ffn_gate, w_ffn_up, w_ffn_down, norm_final):
    splits = [POOL_WIDTH,
              POOL_WIDTH + Q_WIDTH,
              POOL_WIDTH + Q_WIDTH + KV_WIDTH,
              POOL_WIDTH + Q_WIDTH + 2 * KV_WIDTH,
              POOL_WIDTH + Q_WIDTH + 2 * KV_WIDTH + D_MODEL]
    h = x
    for l in range(DEPTH):
        u = rms_norm_2(h, norm_mix[l])
        proj = u @ w_in[l]
        z_pool, q, k, v, g_pool, g_attn = jnp.split(proj, splits, axis=-1)
        y_pool = multiscale_pool(z_pool, w_pool_group[l], pool_scale[l]) @ w_pool_branch[l]
        y_attn = windowed_gqa(q, k, v, sink[l]) @ w_attn_branch[l]
        merged = jax.nn.sigmoid(g_pool) * y_pool + jax.nn.sigmoid(g_attn) * y_attn
        h = h + merged @ w_out[l]
        u = rms_norm_2(h, norm_ffn[l])
        h = h + (jax.nn.silu(u @ w_ffn_gate[l]) * (u @ w_ffn_up[l])) @ w_ffn_down[l]
    return rms_norm_2(h, norm_final)


def setup_inputs(seed=0):
    out = dict(first_inputs(seed))
    for name, value in second_inputs(seed + 1).items():
        if name != "x":
            out[name + "_2"] = value
    return out


def reference(
    x, positions, meta_tokens, pre_mix_norm, w_in, q_norm, w_uq, kv_norm, w_ukv, conv_w,
    attn_out_norm, conv_out_norm, w_out, post_mix_norm, pre_ffn_norm, w_group_router,
    b_group_router, w_expert_router, b_expert_router, w_gate, w_up, w_down, w_sh_gate, w_sh_up,
    w_sh_down, post_ffn_norm, norm_mix_2, w_in_2, w_pool_group_2, pool_scale_2, sink_2,
    w_pool_branch_2, w_attn_branch_2, w_out_2, norm_ffn_2, w_ffn_gate_2, w_ffn_up_2,
    w_ffn_down_2, norm_final_2,
):
    x = first_block(
        x, positions, meta_tokens, pre_mix_norm, w_in, q_norm, w_uq, kv_norm, w_ukv, conv_w,
        attn_out_norm, conv_out_norm, w_out, post_mix_norm, pre_ffn_norm, w_group_router,
        b_group_router, w_expert_router, b_expert_router, w_gate, w_up, w_down, w_sh_gate,
        w_sh_up, w_sh_down, post_ffn_norm,
    )
    return second_block(
        x, norm_mix_2, w_in_2, w_pool_group_2, pool_scale_2, sink_2, w_pool_branch_2,
        w_attn_branch_2, w_out_2, norm_ffn_2, w_ffn_gate_2, w_ffn_up_2, w_ffn_down_2,
        norm_final_2,
    )


_drawn_inputs = setup_inputs


def setup_inputs(seed=0):
    import zlib

    import numpy as np

    out = dict(_drawn_inputs(seed))
    spreads = {}
    factors = {'b_group_router': 4.423,
     'b_expert_router': 2.716,
     'norm_mix_2': 3.51,
     'pool_scale_2': 4.219,
     'sink_2': 64.0,
     'norm_ffn_2': 8.0}
    for name, (base, spread) in spreads.items():
        noise = np.random.default_rng([zlib.crc32(name.encode()), seed]).standard_normal(out[name].shape)
        drawn = base * np.exp(spread * noise) if base else spread * noise
        out[name] = __import__('jax').numpy.asarray(drawn.astype(out[name].dtype))
    for name, factor in factors.items():
        out[name] = (out[name] * factor).astype(out[name].dtype)
    return out
```

```python
from contextlib import ExitStack

import concourse.bass as bass
from concourse import mybir

F32 = mybir.dt.float32
F32R = mybir.dt.float32r
I32 = mybir.dt.int32
ALU = mybir.AluOpType
ACT = mybir.ActivationFunctionType
AX = mybir.AxisListType

P = 128
D = 1024
DT = D // P
TOK = 256
NT = TOK // P
META = 16
COLS = META + TOK
EPS = 1e-6
BIG = 1e30

HEADS = 8
NOPE, ROPE, VD = 64, 32, 64
QKD = NOPE + ROPE
QL, KVL = 256, 128
ZA = QL + KVL + ROPE
CT = 512 // P
ATTN_SCALE = QKD ** -0.5

GROUPS, PER_GROUP, EXPERTS, FF = 4, 8, 32, 256
CAP = 64
PAIRS = PER_GROUP // 2

POOL_WINDOWS = (2, 4, 8, 16)
PAD = 8
HD = 64
FF2 = 2816
F2T = FF2 // P

SLOTS = 8
SLOT = 2048
B1 = 17
MOE_GROUP = 3 * PER_GROUP
B2 = 22
FFN_SLOTS = 3 * F2T // 2
STREAM = B1 + GROUPS * MOE_GROUP + B2 + FFN_SLOTS

C_ID = 0
C_MASK = C_ID + P
C_TRI = C_MASK + COLS
C_ONE = C_TRI + P
C_IOTA = C_ONE + P
C_DESC = C_IOTA + CAP
C_DIST = C_DESC + EXPERTS
C_CNT = C_DIST + NT * TOK
C_FREQ = C_CNT + 4 * TOK
C_POS = C_FREQ + ROPE // 2
C_NHALF = C_POS + 1
CN = C_NHALF + 1

V_GMIX = 0
V_GQ = V_GMIX + DT
V_GKV = V_GQ + QL // P
V_CONV = V_GKV + 1
V_GATT = V_CONV + 3 * CT
V_GCONV = V_GATT + CT
V_GFFN = V_GCONV + CT
V_GMIX2 = V_GFFN + DT
V_GFFN2 = V_GMIX2 + DT
V_PSC = V_GFFN2 + DT
V_RB = V_PSC + 4
V_SINK = V_RB + GROUPS + EXPERTS
V_ROUTE = V_SINK + HEADS
V_PG = V_ROUTE + DT * (GROUPS + EXPERTS)
VN = V_PG + 4 * P

TWO_PI = 6.283185307179586
PI_1 = 6.28125
PI_2 = 0.0019350051879882812
PI_3 = TWO_PI - PI_1 - PI_2
ROUND_MAGIC = 12582912.0
PI_F32 = 3.1415925


def two_blocks(nc, x, meta, consts, small, gains, positions, stream, out):
    ctx = ExitStack()
    with ctx:
        def sb(name, shape, dt=F32):
            return ctx.enter_context(nc.sbuf_tensor(name, shape, dt))

        def sem(name):
            return ctx.enter_context(nc.semaphore(name))

        ring = sb("ring", [P, SLOTS, SLOT])
        h = sb("h", [P, NT, D])
        cst = sb("cst", [P, CN])
        vec = sb("vec", [P, VN])
        gain = sb("gain", [P, 2, D])
        stat = sb("stat", [P, 160])
        pos_i = sb("pos_i", [P, NT], I32)
        rounds_i = sb("rounds_i", [P, 1], I32)

        xh = sb("xh", [P, NT, D], F32R)
        xl = sb("xl", [P, NT, D], F32R)
        sel = sb("sel", [P, NT, PER_GROUP * CAP], F32R)
        selT = sb("selT", [P, PAIRS, TOK], F32R)
        yh = sb("yh", [P, D], F32R)
        yl = sb("yl", [P, D], F32R)

        work = sb("work", [P, 18432])
        top = [0]

        def cut(*shape):
            n = 1
            for s in shape:
                n *= s
            a = work[:, top[0]:top[0] + n]
            top[0] += n
            assert top[0] <= 18432, top
            if len(shape) == 2:
                return a.rearrange("p (a b) -> p a b", b=shape[1])
            return a

        ps = ctx.enter_context(nc.psum_tensor("ps", [P, 8, 512], F32))

        ident = cst[:, C_ID:C_ID + P]
        ones = cst[:, C_ONE:C_ONE + P]
        tri = cst[:, C_TRI:C_TRI + P]
        mask = cst[:, C_MASK:C_MASK + COLS]

        def scol(n):
            a = top_stat[0]
            top_stat[0] += n
            return stat[:, a:a + n]
        top_stat = [0]

        xn = cut(NT + 1, D)
        xT = cut(DT, COLS)
        zt = cut(NT + 1, ZA)
        kr = cut(NT + 1, QKD)
        tabs = cut(8, 3 * ROPE // 2)
        cqT = cut(QL // P, TOK)
        ckvT = cut(COLS)
        qtok = cut(NT, HEADS * QKD)
        qT = cut(HEADS, TOK)
        kT = cut(HEADS, COLS)
        v1 = cut(NT + 1, HEADS * VD)
        mrg = cut(2 * CT, TOK)
        sq = xn.rearrange("p a b -> p (a b)")[:, 0:2 * CT * TOK].rearrange("p (a b) -> p a b", b=TOK)
        rt = cut(4, HEADS * ROPE // 2)
        meta_raw = mrg.rearrange("p a b -> p (a b)")[0:META, 0:D]
        gct = qtok.rearrange("p a b -> p (a b)")[:, 0:2 * COLS].rearrange("p (a b) -> p a b", b=COLS)
        u_t = qT.rearrange("p a b -> p (a b)")[:, 0:COLS]
        cy = qT.rearrange("p a b -> p (a b)")[:, COLS:COLS + TOK]
        pm1 = xT.rearrange("p a b -> p (a b)")[:, 0:3 * COLS].rearrange("p (a b) -> p a b", b=COLS)
        pt1 = xT.rearrange("p a b -> p (a b)")[:, 3 * COLS:3 * COLS + 2 * 384].rearrange("p (a b) -> p a b", b=384)
        mix = qT.rearrange("p a b -> p (a b)").rearrange("p (a b) -> p a b", b=D)
        top[0] = 0

        xn1 = cut(NT, D)
        tT = cut(DT, TOK)
        xg = cut(DT, PER_GROUP * CAP)
        mixb = cut(NT, D)
        sg_s = cut(2, TOK)
        hs = cut(2, TOK)
        sg = cut(FF)
        htok = cut(FF)
        hid = cut(FF // P, P)
        route = cut(24, NT * EXPERTS)
        logit = cut(NT, GROUPS + EXPERTS)
        rankp = cut(NT, EXPERTS + PER_GROUP)
        comb = cut(NT, EXPERTS)
        chosen = cut(NT, EXPERTS)
        wsl = cut(PAIRS)
        cnt = cut(EXPERTS)
        top[0] = 0

        xn2 = cut(NT, D)
        uT = cut(DT, TOK)
        zp = cut(4, TOK + 2 * PAD)
        win = cut(2, TOK + 2 * PAD)
        dp = cut(4, TOK)
        yp = cut(4, TOK)
        q2T = cut(CT, TOK)
        k2T = cut(2, TOK)
        v2 = cut(NT, P)
        gate = cut(DT, 2 * TOK)
        mg = cut(DT, TOK)
        at2 = cut(CT, TOK)
        pm2 = cut(3, TOK)
        pt2 = cut(2, TOK)
        fsg = gate.rearrange("p a b -> p (a b)")[:, 0:4 * TOK].rearrange("p (a b) -> p a b", b=TOK)
        fh = gate.rearrange("p a b -> p (a b)")[:, 4 * TOK:8 * TOK].rearrange("p (a b) -> p a b", b=TOK)

        ssx, msx, rsx = scol(3), scol(3), scol(3)
        ssz, msz, rsz = scol(5), scol(5), scol(5)
        nmx, psum_, rinv = scol(16), scol(16), scol(16)
        msm, rsm = scol(4), scol(4)
        ssa, msa, rsa = scol(2), scol(2), scol(2)
        ssb, msb, rsb = scol(2), scol(2), scol(2)
        ssc, msc, rsc = scol(2), scol(2), scol(2)
        ssd, msd, rsd = scol(2), scol(2), scol(2)
        sse, mse, rse = scol(2), scol(2), scol(2)
        ssf, msf, rsf = scol(2), scol(2), scol(2)
        nsink = scol(HEADS)
        esink = scol(16)
        posf = scol(3)

        x_in, const_in, gain_in, out_st = sem("x_in"), sem("const_in"), sem("gain_in"), sem("out_st")
        full = [sem(f"slot_full{i}") for i in range(SLOTS)]
        full2 = [sem(f"slot2_full{i}") for i in range(SLOTS)]
        used, used2 = sem("slots_used"), sem("slots2_used")
        names = """init ss_done rs_done xn_done turn_ps turn_act turn_dve z_ps z_sb rz_done zn_done kr_done
            conv_ps gc_sb conv_done convg_done t3_ps c_sb kr_sb q_ps q_sb kn_ps kn_sb v_ps v_sb qr_done
            qt_ps qt_act qt_dve s_ps s_sb nm_done e_done p_done pt_ps pt_sb o_ps sq_done ssm_ps msm_done
            rsm_done mix_ps mixa_sb mix_done h1_done xh_done xl_done lg_ps route_a route_b route_c route_d
            chosen_done rank_ps rounds_done sgu_ps ssg_done hs_done dve_step pool_step sin_in tab_done
            sel_done rank_step st_ps st_sb xg_ps xg_act xg_dve gu_ps sg_done ht_done ht_ps hid_done y_ps yh_done yl_done
            moe_done h2_done z2_ps z2_sb q2_ps q2_sb k2_ps k2_sb v2_ps v2_sb g_ps g_sb zpad_done dp_done
            yp_ps yp_sb s2_ps s2_sb nm2_done e2_done p2_done pt2_ps pt2_sb o2_ps o2_sb sig_done br_ps br_sb
            mg_done h3_ps h3_done f_ps fsg_done fh_done facc_ps h4_done y_done""".split()
        s = {n: sem(n) for n in names}

        def slot_ready(eng, n):
            eng.wait_ge(full[n % SLOTS], 16 * (n // SLOTS + 1))

        def slot2_ready(eng, n):
            eng.wait_ge(full2[n % SLOTS], 16 * (n // SLOTS + 1))

        def place2(n):
            return (B1 + GROUPS * MOE_GROUP + n) % SLOTS

        def two_banks(b):
            return ps[:, b:b + 2, :].rearrange("p a b -> p (a b)")

        def conv_bank(m, kind):
            return ((3, 4, 5), (6, 7, 0))[m % 2][kind]

        def gather_bank(t):
            return (7, 4, 5, 6)[t % 4]

        def attention_out(act, hp):
            act.wait_ge(s["o_ps"], 4 * (hp + 1))
            act.activation(mrg[:, hp, :], ps[:, 6 + hp % 2, 0:TOK], ACT.Copy, scale=vec[:, V_GATT + hp:V_GATT + hp + 1])
            act.activation(sq[:, hp, :], ps[:, 6 + hp % 2, 0:TOK], ACT.Square).then_inc(s["sq_done"], 1)

        def attention2_out(act, hp):
            act.wait_ge(s["o2_ps"], 4 * (hp + 1))
            act.activation(at2[:, hp, :], ps[:, 6 + hp % 2, 0:TOK], ACT.Copy).then_inc(s["o2_sb"], 1)

        def gate_out(act, m):
            act.wait_ge(s["g_ps"], m + 1)
            act.activation(gate[:, m, :], ps[:, m % 2, :], ACT.Copy).then_inc(s["g_sb"], 1)

        TILES = [(0, META, 0), (1, P, META), (2, P, META + P)]

        block = ctx.enter_context(nc.Block())

        @block.sync
        def _(sp):
            sp.dma_start(h[:, 0, :], x[0:P, :]).then_inc(x_in, 16)
            sp.dma_start(h[:, 1, :], x[P:TOK, :]).then_inc(x_in, 16)
            sp.dma_start(meta_raw, meta).then_inc(x_in, 16)
            for n in range(B1):
                if n >= SLOTS:
                    sp.wait_ge(used, n - SLOTS + 1)
                sp.dma_start(ring[:, n % SLOTS, :], stream[n]).then_inc(full[n % SLOTS], 16)
            sp.wait_ge(s["rounds_done"], 1)
            rounds = sp.value_load(rounds_i[0:1, 0:1], min_val=1, max_val=GROUPS)
            with sp.Fori(0, rounds) as r:
                with sp.Fori(0, GROUPS) as g:
                    for k in range(MOE_GROUP):
                        n = B1 + k
                        sp.wait_ge(used, (r * GROUPS + g) * MOE_GROUP + (n - SLOTS + 1))
                        sp.dma_start(ring[:, n % SLOTS, :],
                                     stream[bass.ds(g * MOE_GROUP + n, 1)].rearrange("a p f -> p (a f)")
                                     ).then_inc(full[n % SLOTS], 16)
            for n in range(B2 + FFN_SLOTS):
                if n < SLOTS:
                    sp.wait_ge(used, rounds * (GROUPS * MOE_GROUP) + (B1 + n - SLOTS + 1))
                else:
                    sp.wait_ge(used2, n - SLOTS + 1)
                sp.dma_start(ring[:, place2(n), :], stream[B1 + GROUPS * MOE_GROUP + n]
                             ).then_inc(full2[n % SLOTS], 16)
            for i in range(NT):
                sp.wait_ge(s["y_done"], i + 1)
                sp.dma_start(out[i * P:(i + 1) * P, :], xn2[:, i, :]).then_inc(out_st, 16)
            sp.wait_ge(out_st, 16 * NT)

        @block.scalar
        def _(act):
            act.dma_start(cst[:], consts).then_inc(const_in, 16)
            act.dma_start(vec[:], small).then_inc(const_in, 16)
            act.dma_start(pos_i[:], positions).then_inc(const_in, 16)
            act.dma_start(gain[:], gains[:, 0:2, :]).then_inc(gain_in, 16)

            act.wait_ge(x_in, 48)
            act.wait_ge(s["init"], 1)
            act.activation(xn[0:META, 0, :], meta_raw, ACT.Square, accum_out=ssx[0:META, 0:1])
            act.activation(xn[:, 1, :], h[:, 0, :], ACT.Square, accum_out=ssx[:, 1:2])
            act.activation(xn[:, 2, :], h[:, 1, :], ACT.Square, accum_out=ssx[:, 2:3]).then_inc(s["ss_done"], 1)

            act.wait_ge(s["sin_in"], 1)
            act.activation(tabs[:, 1, :], tabs[:, 4, :], ACT.Sin)
            act.activation(tabs[:, 0, :], tabs[:, 5, :], ACT.Sin).then_inc(s["tab_done"], 1)

            for t in range(0, DT, 2):
                act.wait_ge(s["turn_ps"], t + 1)
                act.activation(xT[:, t, :], ps[:, t, 0:COLS], ACT.Copy,
                               scale=vec[:, V_GMIX + t:V_GMIX + t + 1]).then_inc(s["turn_act"], 1)

            for i, m, _ in TILES:
                act.wait_ge(s["z_ps"], i + 1)
                act.activation(xn[0:m, i, 0:KVL], ps[0:m, i, QL:QL + KVL], ACT.Square, accum_out=ssz[0:m, i:i + 1])
                if i:
                    act.activation(xn[0:m, i, KVL:KVL + QL], ps[0:m, i, 0:QL], ACT.Square,
                                   accum_out=ssz[0:m, 2 + i:3 + i])
                act.activation(zt[0:m, i, :], ps[0:m, i, 0:ZA], ACT.Copy).then_inc(s["z_sb"], 1)

            for m in range(CT):
                act.wait_ge(s["conv_ps"], 3 * m + 1)
                if m >= 2:
                    act.wait_ge(s["conv_done"], m - 1)
                act.activation(gct[:, m % 2, :], ps[:, conv_bank(m, 0), 0:COLS], ACT.Copy).then_inc(s["gc_sb"], 1)
                if m:
                    act.wait_ge(s["conv_done"], m)
                    act.activation(sq[:, CT + m - 1, :], mrg[:, CT + m - 1, :], ACT.Square).then_inc(s["sq_done"], 1)
            act.wait_ge(s["conv_done"], CT)
            act.activation(sq[:, 2 * CT - 1, :], mrg[:, 2 * CT - 1, :], ACT.Square).then_inc(s["sq_done"], 1)

            act.wait_ge(s["t3_ps"], 1)
            for f in range(QL // P):
                act.activation(cqT[:, f, :], ps[:, 1, f * TOK:(f + 1) * TOK], ACT.Copy,
                               scale=vec[:, V_GQ + f:V_GQ + f + 1]).then_inc(s["c_sb"], 1)
            act.wait_ge(s["t3_ps"], 2)
            act.activation(ckvT, ps[:, 2, 0:COLS], ACT.Copy, scale=vec[:, V_GKV:V_GKV + 1]).then_inc(s["c_sb"], 1)

            for i in range(NT):
                act.wait_ge(s["q_ps"], i + 1)
                act.activation(qtok[:, i, :], two_banks(4 + 2 * i)[:, 0:HEADS * QKD], ACT.Copy).then_inc(s["q_sb"], 1)
            for i, m in enumerate((P, P, META)):
                act.wait_ge(s["v_ps"], i + 1)
                act.activation(v1[0:m, i, :], ps[0:m, 4 + i, :], ACT.Copy).then_inc(s["v_sb"], 1)
            for hp in range(0, HEADS // 2, 2):
                act.wait_ge(s["qt_ps"], hp + 1)
                act.activation(qT[0:QKD, 2 * hp:2 * hp + 2, :], ps[0:QKD, hp, :].rearrange("p (a b) -> p a b", b=TOK),
                               ACT.Copy).then_inc(s["qt_act"], 1)

            for u in range(2 * HEADS + 1):
                if u < 2 * HEADS:
                    nk = META + P if u % 2 == 0 else COLS
                    act.wait_ge(s["nm_done"], u + 1)
                    act.activation(pm1[:, u % 3, 0:nk], pm1[:, u % 3, 0:nk], ACT.Exp, bias=nmx[:, u:u + 1],
                                   accum_out=psum_[:, u:u + 1]).then_inc(s["e_done"], 1)
                if u:
                    w = u - 1
                    act.wait_ge(s["pt_ps"], w + 1)
                    full_k = P if w % 2 == 0 else 2 * P
                    act.activation(pt1[:, w % 2, 0:full_k], ps[:, 3 + w % 2, 0:full_k], ACT.Copy)
                    act.activation(pt1[0:META, w % 2, full_k:full_k + P], ps[0:META, 3 + w % 2, full_k:full_k + P],
                                   ACT.Copy).then_inc(s["pt_sb"], 1)
                    if w >= 4 and w % 4 == 0:
                        attention_out(act, w // 4 - 1)
            attention_out(act, CT - 1)

            act.wait_ge(s["rsm_done"], 1)
            for j in range(2 * NT):
                i, n = j // 2, j % 2
                act.wait_ge(s["mix_ps"], j + 1)
                act.activation(mix[:, i, n * 512:(n + 1) * 512], ps[:, 4 * i + n, :], ACT.Copy,
                               scale=rsm[:, 2 * i:2 * i + 1]).then_inc(s["mixa_sb"], 1)
            for i in range(NT):
                act.wait_ge(s["mix_done"], 2 * i + 2)
                act.activation(xn1[:, i, :], mix[:, i, :], ACT.Square, accum_out=ssa[:, i:i + 1]).then_inc(s["ss_done"], 1)
            for i in range(NT):
                act.wait_ge(s["h1_done"], i + 1)
                act.activation(xn1[:, i, :], h[:, i, :], ACT.Square, accum_out=ssb[:, i:i + 1]).then_inc(s["ss_done"], 1)
            for i in range(NT):
                act.wait_ge(s["xn_done"], 1 + i + 1)
                act.activation(xh[:, i, :], xn1[:, i, :], ACT.Copy).then_inc(s["xh_done"], 1)
            for t in range(0, DT, 2):
                act.wait_ge(s["turn_ps"], 8 + t + 1)
                act.activation(tT[:, t, :], ps[:, t, 0:TOK], ACT.Copy,
                               scale=vec[:, V_GFFN + t:V_GFFN + t + 1]).then_inc(s["turn_act"], 1)

            act.wait_ge(s["route_a"], 1)
            act.activation(route[:, 1, 0:NT * GROUPS], route[:, 1, 0:NT * GROUPS], ACT.Exp).then_inc(s["route_b"], 1)
            act.wait_ge(s["route_c"], 1)
            act.activation(route[:, 12, 0:NT], route[:, 12, 0:NT], ACT.Exp).then_inc(s["route_d"], 1)

            for f in range(2):
                act.wait_ge(s["sgu_ps"], f + 1)
                act.activation(sg_s[:, f, :], ps[:, 4 + f, 0:TOK], ACT.Silu).then_inc(s["ssg_done"], 1)

            act.wait_ge(s["rounds_done"], 1)
            rounds = act.value_load(rounds_i[0:1, 0:1], min_val=1, max_val=GROUPS)
            with act.Fori(0, rounds) as r:
                with act.Fori(0, GROUPS) as g:
                    it = act.snap(r * GROUPS + g)
                    for t in range(0, DT, 2):
                        act.wait_ge(s["xg_ps"], it * DT + (t + 1))
                        act.activation(xg[:, t, :], ps[:, gather_bank(t), :], ACT.Copy,
                                       scale=vec[:, V_GFFN + t:V_GFFN + t + 1]).then_inc(s["xg_act"], 1)
                    for p in range(PAIRS + 1):
                        if p < PAIRS:
                            act.wait_ge(s["gu_ps"], it * PAIRS + (p + 1))
                            act.activation(sg, ps[:, 4 + p % 2, 0:FF], ACT.Silu).then_inc(s["sg_done"], 1)
                        if p:
                            for n in range(2):
                                act.wait_ge(s["y_ps"], it * (2 * PAIRS) + (2 * (p - 1) + n + 1))
                                act.activation(yh[:, n * 512:(n + 1) * 512], ps[:, 6 + n, :], ACT.Copy,
                                               scale=wsl[:, p - 1:p]).then_inc(s["yh_done"], 1)
                        if p < PAIRS:
                            act.wait_ge(s["ht_ps"], it * PAIRS + (p + 1))
                            act.activation(hid, ps[:, 4 + p % 2, 0:FF].rearrange("p (a b) -> p a b", b=P), ACT.Copy
                                           ).then_inc(s["hid_done"], 1)

            act.wait_ge(s["moe_done"], rounds * GROUPS)
            for i in range(NT):
                act.activation(mixb[:, i, :], two_banks(2 * i), ACT.Square, accum_out=ssc[:, i:i + 1]).then_inc(s["ss_done"], 1)
            for i in range(NT):
                act.wait_ge(s["h2_done"], i + 1)
                act.activation(xn2[:, i, :], h[:, i, :], ACT.Square, accum_out=ssd[:, i:i + 1]).then_inc(s["ss_done"], 1)
            act.dma_start(gain[:, 0, :], gains[:, 2, :]).then_inc(gain_in, 16)
            for t in range(0, DT, 2):
                act.wait_ge(s["turn_ps"], 16 + t + 1)
                act.activation(uT[:, t, :], ps[:, t, 0:TOK], ACT.Copy,
                               scale=vec[:, V_GMIX2 + t:V_GMIX2 + t + 1]).then_inc(s["turn_act"], 1)

            act.wait_ge(s["zpad_done"], 1)
            for c in range(4):
                act.wait_ge(s["z2_ps"], c + 1)
                act.activation(zp[:, c, PAD:PAD + TOK], ps[:, c, 0:TOK], ACT.Copy).then_inc(s["z2_sb"], 1)
            for c in range(CT):
                act.wait_ge(s["q2_ps"], c + 1)
                act.activation(q2T[:, c, :], ps[:, 4 + c, 0:TOK], ACT.Copy, scale=HD ** -0.5).then_inc(s["q2_sb"], 1)
            for c in range(2):
                act.wait_ge(s["k2_ps"], c + 1)
                act.activation(k2T[:, c, :], ps[:, c, 0:TOK], ACT.Copy).then_inc(s["k2_sb"], 1)
            act.wait_ge(s["v2_ps"], 1)
            act.activation(v2, ps[:, 2, 0:2 * P].rearrange("p (a b) -> p a b", b=P), ACT.Copy).then_inc(s["v2_sb"], 1)

            for u in range(2 * HEADS + 1):
                if u < 2 * HEADS:
                    hd = u // 2
                    act.wait_ge(s["nm2_done"], u + 1)
                    act.activation(pm2[:, u % 3, :], pm2[:, u % 3, :], ACT.Exp, bias=nmx[:, u:u + 1],
                                   accum_out=psum_[:, u:u + 1])
                    act.activation(esink[:, u:u + 1], vec[:, V_SINK + hd:V_SINK + hd + 1], ACT.Exp,
                                   bias=nmx[:, u:u + 1]).then_inc(s["e2_done"], 1)
                if u:
                    w = u - 1
                    act.wait_ge(s["pt2_ps"], w + 1)
                    act.activation(pt2[:, w % 2, :], ps[:, 4 + w % 2, 0:TOK], ACT.Copy).then_inc(s["pt2_sb"], 1)
                    if w >= 4 and w % 4 == 0:
                        attention2_out(act, w // 4 - 1)
                    if w % 2 == 1:
                        gate_out(act, w // 2)
            attention2_out(act, CT - 1)
            for m in range(DT):
                act.wait_ge(s["g_sb"], m + 1)
                act.activation(gate[:, m, :], gate[:, m, :], ACT.Sigmoid).then_inc(s["sig_done"], 1)
                if m < 4:
                    act.wait_ge(s["yp_ps"], m + 1)
                    act.activation(yp[:, m, :], ps[:, m % 2, 0:TOK], ACT.Copy,
                                   scale=vec[:, V_PSC + m:V_PSC + m + 1]).then_inc(s["yp_sb"], 1)
            for i in range(NT):
                act.wait_ge(s["h3_done"], i + 1)
                act.activation(xn2[:, i, :], h[:, i, :], ACT.Square, accum_out=sse[:, i:i + 1]).then_inc(s["ss_done"], 1)
            for t in range(0, DT, 2):
                act.wait_ge(s["turn_ps"], 24 + t + 1)
                act.activation(uT[:, t, :], ps[:, t, 0:TOK], ACT.Copy,
                               scale=vec[:, V_GFFN2 + t:V_GFFN2 + t + 1]).then_inc(s["turn_act"], 1)

            for m in range(F2T):
                act.wait_ge(s["f_ps"], m + 1)
                act.activation(fsg[:, m % 4, :], ps[:, 4 + m % 4, 0:TOK], ACT.Silu).then_inc(s["fsg_done"], 1)
            for i in range(NT):
                act.wait_ge(s["h4_done"], i + 1)
                act.activation(xn2[:, i, :], h[:, i, :], ACT.Square, accum_out=ssf[:, i:i + 1]).then_inc(s["ss_done"], 1)

        @block.gpsimd
        def _(pool):
            steps = [0]

            def rstd(ss, ms, rs, n, done):
                pool.tensor_scalar(ms, ss, 1.0 / n, EPS, ALU.mult, ALU.add).then_inc(s["pool_step"], 1)
                steps[0] += 1
                pool.wait_ge(s["pool_step"], steps[0])
                power(ms, rs).then_inc(done, 1)

            def power(ms, rs):
                return pool.tensor_tensor(rs, ms, cst[:, C_NHALF:C_NHALF + 1].to_broadcast([P, rs.shape[1]]), ALU.pow)

            pool.wait_ge(const_in, 48)
            pool.wait_ge(s["ss_done"], 1)
            rstd(ssx, msx, rsx, D, s["rs_done"])
            pool.wait_ge(s["z_sb"], 3)
            pool.tensor_scalar(msz[:, 0:3], ssz[:, 0:3], 1.0 / KVL, EPS, ALU.mult, ALU.add).then_inc(s["pool_step"], 1)
            pool.tensor_scalar(msz[:, 3:5], ssz[:, 3:5], 1.0 / QL, EPS, ALU.mult, ALU.add).then_inc(s["pool_step"], 1)
            steps[0] += 2
            pool.wait_ge(s["pool_step"], steps[0])
            power(msz, rsz).then_inc(s["rz_done"], 1)
            for m in range(CT):
                pool.wait_ge(s["sq_done"], m + 1)
                pool.tensor_scalar(mrg[:, CT + m, :], mrg[:, CT + m, :], vec[:, V_GCONV + m:V_GCONV + m + 1], 1.0,
                                   ALU.mult, ALU.mult).then_inc(s["convg_done"], 1)
            pool.wait_ge(s["msm_done"], 1)
            power(msm, rsm).then_inc(s["rsm_done"], 1)
            for k, (ss, ms, rs) in enumerate(((ssa, msa, rsa), (ssb, msb, rsb), (ssc, msc, rsc), (ssd, msd, rsd))):
                for i in range(NT):
                    pool.wait_ge(s["ss_done"], 1 + NT * k + i + 1)
                    rstd(ss[:, i:i + 1], ms[:, i:i + 1], rs[:, i:i + 1], D, s["rs_done"])

            for c, w in enumerate(POOL_WINDOWS):
                pool.wait_ge(s["z2_sb"], c + 1)
                src, half, k, wide = zp[:, c, :], 1, 0, TOK + 2 * PAD
                while half < w:
                    back, ahead = (1, 0) if half == 1 else (half // 2, half // 2)
                    lo, hi = half, wide - half + 1
                    pool.tensor_tensor(win[:, k % 2, lo:hi], src[:, lo - back:hi - back],
                                       src[:, lo + ahead:hi + ahead], ALU.add).then_inc(s["pool_step"], 1)
                    steps[0] += 1
                    pool.wait_ge(s["pool_step"], steps[0])
                    src, half, k = win[:, k % 2, :], 2 * half, k + 1
                pool.tensor_tensor(dp[:, c, :], src[:, PAD:PAD + TOK], cst[:, C_CNT + c * TOK:C_CNT + (c + 1) * TOK],
                                   ALU.mult).then_inc(s["pool_step"], 1)
                steps[0] += 1
                pool.wait_ge(s["pool_step"], steps[0])
                pool.tensor_tensor(dp[:, c, :], dp[:, c, :], zp[:, c, PAD:PAD + TOK], ALU.subtract).then_inc(s["dp_done"], 1)
            for k, (ss, ms, rs) in enumerate(((sse, mse, rse), (ssf, msf, rsf))):
                for i in range(NT):
                    pool.wait_ge(s["ss_done"], 1 + NT * (4 + k) + i + 1)
                    rstd(ss[:, i:i + 1], ms[:, i:i + 1], rs[:, i:i + 1], D, s["rs_done"])

        @block.vector
        def _(dve):
            steps = [0]

            def link(ins):
                ins.then_inc(s["dve_step"], 1)
                steps[0] += 1
                dve.wait_ge(s["dve_step"], steps[0])

            def halves(a, w):
                return a.rearrange("p (a b) -> p a b", b=w)

            dve.memset(stat[:], 1.0)
            dve.memset(zt[:, 0, :], 0.0)
            dve.memset(kr, 0.0).then_inc(s["init"], 1)

            dve.wait_ge(const_in, 48)
            dve.wait_ge(s["init"], 1)
            dve.tensor_copy(posf[:, 0:1], cst[:, C_POS:C_POS + 1])
            link(dve.tensor_copy(posf[:, 1:3], pos_i[:]))
            link(dve.tensor_scalar(posf[:, 1:3], posf[:, 1:3], float(META), None, ALU.add))
            NR = ROPE // 2
            ang, kk, red, co, ab = (tabs[:, j, :] for j in (2, 3, 4, 5, 6))
            link(dve.tensor_tensor(halves(ang, NR), cst[:, C_FREQ:C_FREQ + NR].unsqueeze(1).to_broadcast([P, 3, NR]),
                                   posf.unsqueeze(2).to_broadcast([P, 3, NR]), ALU.mult))
            link(dve.tensor_scalar(kk, ang, 1.0 / TWO_PI, ROUND_MAGIC, ALU.mult, ALU.add))
            link(dve.tensor_scalar(kk, kk, -ROUND_MAGIC, None, ALU.add))
            link(dve.scalar_tensor_tensor(red, kk, -PI_1, ang, ALU.mult, ALU.add))
            link(dve.scalar_tensor_tensor(red, kk, -PI_2, red, ALU.mult, ALU.add))
            link(dve.scalar_tensor_tensor(red, kk, -PI_3, red, ALU.mult, ALU.add))
            link(dve.tensor_scalar(red, red, PI_F32, -PI_F32, ALU.min, ALU.max))
            link(dve.scalar_tensor_tensor(ab, red, -1.0, red, ALU.mult, ALU.min))
            dve.tensor_scalar(co, ab, TWO_PI / 4, None, ALU.add).then_inc(s["sin_in"], 1)

            dve.wait_ge(s["rs_done"], 1)
            dve.tensor_scalar(xn[0:META, 0, :], meta_raw, rsx[0:META, 0:1], None, ALU.mult)
            for i in range(NT):
                last = dve.tensor_scalar(xn[:, 1 + i, :], h[:, i, :], rsx[:, 1 + i:2 + i], None, ALU.mult)
            last.then_inc(s["xn_done"], 1)
            for t in range(1, DT, 2):
                dve.wait_ge(s["turn_ps"], t + 1)
                dve.tensor_scalar(xT[:, t, :], ps[:, t, 0:COLS], vec[:, V_GMIX + t:V_GMIX + t + 1], None,
                                  ALU.mult).then_inc(s["turn_dve"], 1)

            def rope(x1, x2, cos, sin, o1, o2, temps):
                a, b, c, d = temps
                dve.tensor_tensor(a, x1, cos, ALU.mult)
                dve.tensor_tensor(b, x2, sin, ALU.mult)
                dve.tensor_tensor(c, x2, cos, ALU.mult)
                link(dve.tensor_tensor(d, x1, sin, ALU.mult))
                dve.tensor_tensor(o1, a, b, ALU.subtract)
                return dve.tensor_tensor(o2, c, d, ALU.add)

            dve.wait_ge(s["z_sb"], 3)
            dve.wait_ge(s["tab_done"], 1)
            z0 = QL + KVL
            rope(zt[:, :, z0:z0 + NR], zt[:, :, z0 + NR:z0 + ROPE], halves(tabs[:, 0, :], NR), halves(tabs[:, 1, :], NR),
                 kr[:, :, NOPE:NOPE + NR], kr[:, :, NOPE + NR:QKD],
                 [halves(rt[:, j, 0:3 * NR], NR) for j in range(4)]).then_inc(s["kr_done"], 1)
            dve.wait_ge(s["rz_done"], 1)
            for i in range(NT + 1):
                last = dve.tensor_scalar(zt[:, i, QL:z0], zt[:, i, QL:z0], rsz[:, i:i + 1], None, ALU.mult)
                if i:
                    last = dve.tensor_scalar(zt[:, i, 0:QL], zt[:, i, 0:QL], rsz[:, 2 + i:3 + i], None, ALU.mult)
            last.then_inc(s["zn_done"], 1)

            for m in range(CT):
                dve.wait_ge(s["gc_sb"], m + 1)
                dve.wait_ge(s["conv_ps"], 3 * m + 2)
                link(dve.tensor_tensor(u_t, gct[:, m % 2, :], ps[:, conv_bank(m, 1), 0:COLS], ALU.mult))
                w = [vec[:, V_CONV + k * CT + m:V_CONV + k * CT + m + 1] for k in range(3)]
                link(dve.tensor_scalar(cy, u_t[:, META - 2:META - 2 + TOK], w[0], None, ALU.mult))
                link(dve.scalar_tensor_tensor(cy, u_t[:, META - 1:META - 1 + TOK], w[1], cy, ALU.mult, ALU.add))
                link(dve.scalar_tensor_tensor(cy, u_t[:, META:META + TOK], w[2], cy, ALU.mult, ALU.add))
                dve.wait_ge(s["conv_ps"], 3 * m + 3)
                dve.tensor_tensor(mrg[:, CT + m, :], cy, ps[:, conv_bank(m, 2), 0:TOK], ALU.mult
                                  ).then_inc(s["conv_done"], 1)

            dve.wait_ge(s["t3_ps"], 3)
            dve.tensor_copy(kT[NOPE:QKD, :, :], ps[NOPE:QKD, 3, 0:COLS].unsqueeze(1).to_broadcast([ROPE, HEADS, COLS])
                            ).then_inc(s["kr_sb"], 1)

            def k_out(hd):
                dve.wait_ge(s["kn_ps"], hd + 1)
                dve.tensor_copy(kT[0:NOPE, hd, :], ps[0:NOPE, hd % 4, 0:COLS]).then_inc(s["kn_sb"], 1)

            def q_rope(i):
                dve.wait_ge(s["q_sb"], i + 1)
                q = halves(qtok[:, i, :], QKD)
                c, sn = (tabs[:, j, (1 + i) * NR:(2 + i) * NR].unsqueeze(1).to_broadcast([P, HEADS, NR]) for j in (0, 1))
                x1, x2 = q[:, :, NOPE:NOPE + NR], q[:, :, NOPE + NR:QKD]
                rope(x1, x2, c, sn, x1, x2, [halves(rt[:, j, :], NR) for j in range(4)]).then_inc(s["qr_done"], 1)

            for hd in range(4):
                k_out(hd)
            q_rope(0)
            for hd in range(4, HEADS):
                k_out(hd)
            dve.wait_ge(s["qr_done"], 1)
            q_rope(1)
            for hp in range(1, HEADS // 2, 2):
                dve.wait_ge(s["qt_ps"], hp + 1)
                dve.tensor_copy(qT[0:QKD, 2 * hp:2 * hp + 2, :], halves(ps[0:QKD, hp, :], TOK)).then_inc(s["qt_dve"], 1)

            for u in range(2 * HEADS + 1):
                if u < 2 * HEADS:
                    nk = META + P if u % 2 == 0 else COLS
                    dve.wait_ge(s["s_ps"], u + 1)
                    dve.scalar_tensor_tensor(pm1[:, u % 3, 0:nk], ps[:, u % 3, 0:nk], ATTN_SCALE, mask[:, COLS - nk:COLS],
                                             ALU.mult, ALU.add).then_inc(s["s_sb"], 1)
                    dve.wait_ge(s["s_sb"], u + 1)
                    dve.tensor_reduce(nmx[:, u:u + 1], pm1[:, u % 3, 0:nk], AX.X, ALU.max, negate=True
                                      ).then_inc(s["nm_done"], 1)
                if u:
                    w = u - 1
                    nk = META + P if w % 2 == 0 else COLS
                    dve.wait_ge(s["e_done"], w + 1)
                    link(dve.reciprocal(rinv[:, w:w + 1], psum_[:, w:w + 1]))
                    dve.tensor_scalar(pm1[:, w % 3, 0:nk], pm1[:, w % 3, 0:nk], rinv[:, w:w + 1], None, ALU.mult
                                      ).then_inc(s["p_done"], 1)

            dve.wait_ge(s["ssm_ps"], 1)
            dve.tensor_scalar(msm, ps[:, 5, 0:4], 1.0 / 512, EPS, ALU.mult, ALU.add).then_inc(s["msm_done"], 1)
            dve.wait_ge(s["rsm_done"], 1)
            for j in range(2 * NT):
                i, n = j // 2, j % 2
                dve.wait_ge(s["mix_ps"], 4 + j + 1)
                dve.wait_ge(s["mixa_sb"], j + 1)
                o = mix[:, i, n * 512:(n + 1) * 512]
                dve.scalar_tensor_tensor(o, ps[:, 4 * i + 2 + n, :], rsm[:, 2 * i + 1:2 * i + 2], o, ALU.mult, ALU.add
                                         ).then_inc(s["mix_done"], 1)

            dve.wait_ge(gain_in, 16)
            for i in range(NT):
                dve.wait_ge(s["rs_done"], 1 + i + 1)
                link(dve.scalar_tensor_tensor(mix[:, i, :], mix[:, i, :], rsa[:, i:i + 1], gain[:, 0, :], ALU.mult, ALU.mult))
                dve.tensor_tensor(h[:, i, :], h[:, i, :], mix[:, i, :], ALU.add).then_inc(s["h1_done"], 1)
            for i in range(NT):
                dve.wait_ge(s["rs_done"], 3 + i + 1)
                dve.tensor_scalar(xn1[:, i, :], h[:, i, :], rsb[:, i:i + 1], None, ALU.mult).then_inc(s["xn_done"], 1)
            for t in range(1, DT, 2):
                dve.wait_ge(s["turn_ps"], 8 + t + 1)
                dve.tensor_scalar(tT[:, t, :], ps[:, t, 0:TOK], vec[:, V_GFFN + t:V_GFFN + t + 1], None,
                                  ALU.mult).then_inc(s["turn_dve"], 1)

            def rt_(k, w):
                a = route[:, k, 0:NT * w]
                return a if w == 1 else halves(a, w)

            def wide(a, w):
                return a.unsqueeze(2).to_broadcast([P, NT, w])

            def first_max(x, k, w):
                desc = cst[:, C_DESC:C_DESC + w].unsqueeze(1).to_broadcast([P, NT, w])
                link(dve.tensor_reduce(rt_(k, 1), x, AX.X, ALU.max))
                link(dve.tensor_tensor(rt_(k + 1, w), x, wide(rt_(k, 1), w), ALU.is_equal))
                link(dve.tensor_tensor(rt_(k + 2, w), rt_(k + 1, w), desc, ALU.mult))
                link(dve.tensor_reduce(rt_(k + 3, 1), rt_(k + 2, w), AX.X, ALU.max))
                link(dve.tensor_tensor(rt_(k + 4, w), rt_(k + 2, w), wide(rt_(k + 3, 1), w), ALU.is_equal))
                return rt_(k, 1), rt_(k + 4, w)

            dve.wait_ge(s["lg_ps"], 1)
            W = GROUPS + EXPERTS
            link(dve.tensor_tensor(logit, halves(ps[:, 6, 0:NT * W], W),
                                   vec[:, V_RB:V_RB + W].unsqueeze(1).to_broadcast([P, NT, W]), ALU.add))
            gl, el = logit[:, :, 0:GROUPS], logit[:, :, GROUPS:W]
            gmax, group = first_max(gl, 2, GROUPS)
            dve.tensor_tensor(rt_(1, GROUPS), gl, wide(gmax, GROUPS), ALU.subtract).then_inc(s["route_a"], 1)
            link(dve.tensor_scalar(rt_(7, GROUPS), group, BIG, -BIG, ALU.mult, ALU.add))
            em = rt_(8, EXPERTS)
            link(dve.tensor_tensor(em.rearrange("p a (b c) -> p a b c", c=PER_GROUP),
                                   el.rearrange("p a (b c) -> p a b c", c=PER_GROUP),
                                   rt_(7, GROUPS).unsqueeze(3).to_broadcast([P, NT, GROUPS, PER_GROUP]), ALU.add))
            m1, h1 = first_max(em, 13, EXPERTS)
            link(dve.scalar_tensor_tensor(rt_(9, EXPERTS), h1, -2 * BIG, em, ALU.mult, ALU.add))
            m2, h2 = first_max(rt_(9, EXPERTS), 18, EXPERTS)
            dve.tensor_tensor(rt_(12, 1), m2, m1, ALU.subtract).then_inc(s["route_c"], 1)
            dve.tensor_tensor(chosen, h1, h2, ALU.add).then_inc(s["chosen_done"], 1)
            dve.wait_ge(s["route_b"], 1)
            link(dve.tensor_reduce(rt_(0, 1), rt_(1, GROUPS), AX.X, ALU.add))
            dve.wait_ge(s["route_d"], 1)
            link(dve.tensor_scalar(rt_(10, 1), rt_(12, 1), 1.0, None, ALU.add))
            link(dve.tensor_tensor(rt_(10, 1), rt_(10, 1), rt_(0, 1), ALU.mult))
            link(dve.reciprocal(rt_(10, 1), rt_(10, 1)))
            link(dve.tensor_tensor(rt_(11, 1), rt_(10, 1), rt_(12, 1), ALU.mult))
            link(dve.tensor_tensor(comb, h1, wide(rt_(10, 1), EXPERTS), ALU.mult))
            link(dve.tensor_tensor(rt_(9, EXPERTS), h2, wide(rt_(11, 1), EXPERTS), ALU.mult))
            link(dve.tensor_tensor(comb, comb, rt_(9, EXPERTS), ALU.add))

            link(dve.tensor_scalar(rankp[:, :, 0:EXPERTS], chosen, -1e4, 1e4, ALU.mult, ALU.add))
            dve.wait_ge(s["rank_ps"], 1)
            link(dve.tensor_tensor(rankp[:, :, 0:EXPERTS], rankp[:, :, 0:EXPERTS], halves(ps[:, 7, 0:NT * EXPERTS], EXPERTS),
                                   ALU.add))
            link(dve.tensor_scalar(rankp[:, :, EXPERTS:EXPERTS + PER_GROUP], rankp[:, :, 0:PER_GROUP], -float(CAP), None,
                                   ALU.add))
            link(dve.tensor_reduce(cnt[:, 0:1], ps[:, 7, NT * EXPERTS:(NT + 1) * EXPERTS], AX.X, ALU.max))
            link(dve.tensor_scalar(cnt[:, 1:2], cnt[:, 0:1], float(CAP), 1.0, ALU.is_gt, ALU.add))
            for k in range(2, TOK // CAP):
                link(dve.scalar_tensor_tensor(cnt[:, k:k + 1], cnt[:, 0:1], float(k * CAP), cnt[:, k - 1:k],
                                              ALU.is_gt, ALU.add))
            dve.tensor_copy(rounds_i[:], cnt[:, TOK // CAP - 1:TOK // CAP]).then_inc(s["rounds_done"], 1)

            for f in range(2):
                dve.wait_ge(s["ssg_done"], f + 1)
                dve.tensor_tensor(hs[:, f, :], sg_s[:, f, :], ps[:, 4 + f, TOK:2 * TOK], ALU.mult).then_inc(s["hs_done"], 1)
            for i in range(NT):
                dve.wait_ge(s["xh_done"], i + 1)
                dve.tensor_tensor(xl[:, i, :], xn1[:, i, :], xh[:, i, :].bitcast(F32), ALU.subtract).then_inc(s["xl_done"], 1)

            def select(ranks):
                for i in range(NT):
                    last = dve.tensor_tensor(
                        halves(sel[:, i, :], CAP), ranks[:, i, :].unsqueeze(2).to_broadcast([P, PER_GROUP, CAP]),
                        cst[:, C_IOTA:C_IOTA + CAP].unsqueeze(1).to_broadcast([P, PER_GROUP, CAP]), ALU.is_equal)
                last.then_inc(s["sel_done"], 1)

            select(rankp[:, :, 0:PER_GROUP])
            dve.wait_ge(s["rounds_done"], 1)
            rounds = dve.value_load(rounds_i[0:1, 0:1], min_val=1, max_val=GROUPS)
            with dve.Fori(0, rounds) as r:
                with dve.Fori(0, GROUPS) as g:
                    it = dve.snap(r * GROUPS + g)
                    for q in range(2):
                        dve.wait_ge(s["st_ps"], it * 3 + (q + 1))
                        dve.tensor_copy(selT[:, 2 * q:2 * q + 2, :], halves(ps[:, 4 + q, :], TOK)).then_inc(s["st_sb"], 1)
                    dve.wait_ge(s["st_ps"], it * 3 + 3)
                    dve.tensor_copy(wsl[0:CAP, :], ps[0:CAP, 6, 0:2 * PAIRS:2])
                    dve.tensor_copy(wsl[CAP:P, :], ps[CAP:P, 6, 1:2 * PAIRS:2]).then_inc(s["st_sb"], 1)
                    for t in range(1, DT, 2):
                        dve.wait_ge(s["xg_ps"], it * DT + (t + 1))
                        dve.tensor_scalar(xg[:, t, :], ps[:, gather_bank(t), :], vec[:, V_GFFN + t:V_GFFN + t + 1], None,
                                          ALU.mult).then_inc(s["xg_dve"], 1)
                    ahead = rankp[:, :, bass.ds(g * PER_GROUP + PER_GROUP, PER_GROUP)]
                    select(ahead)
                    dve.wait_ge(s["sel_done"], it + 2)
                    dve.tensor_scalar(ahead, ahead, -float(CAP), None, ALU.add).then_inc(s["rank_step"], 1)
                    for p in range(PAIRS + 1):
                        if p < PAIRS:
                            dve.wait_ge(s["sg_done"], it * PAIRS + (p + 1))
                            dve.tensor_tensor(htok, sg, ps[:, 4 + p % 2, FF:2 * FF], ALU.mult).then_inc(s["ht_done"], 1)
                        if p:
                            for n in range(2):
                                dve.wait_ge(s["yh_done"], it * (2 * PAIRS) + (2 * (p - 1) + n + 1))
                                dve.scalar_tensor_tensor(yl[:, n * 512:(n + 1) * 512], ps[:, 6 + n, :], wsl[:, p - 1:p],
                                                         yh[:, n * 512:(n + 1) * 512].bitcast(F32), ALU.mult, ALU.subtract
                                                         ).then_inc(s["yl_done"], 1)
                    dve.wait_ge(s["rank_step"], it + 1)

            for i in range(NT):
                dve.wait_ge(s["rs_done"], 5 + i + 1)
                link(dve.scalar_tensor_tensor(mixb[:, i, :], two_banks(2 * i), rsc[:, i:i + 1], gain[:, 1, :], ALU.mult, ALU.mult))
                dve.tensor_tensor(h[:, i, :], h[:, i, :], mixb[:, i, :], ALU.add).then_inc(s["h2_done"], 1)
            for i in range(NT):
                dve.wait_ge(s["rs_done"], 7 + i + 1)
                dve.tensor_scalar(xn2[:, i, :], h[:, i, :], rsd[:, i:i + 1], None, ALU.mult).then_inc(s["xn_done"], 1)
            dve.tensor_scalar(nsink, vec[:, V_SINK:V_SINK + HEADS], -1.0, None, ALU.mult)
            dve.memset(win, 0.0)
            dve.memset(zp, 0.0).then_inc(s["zpad_done"], 1)
            for t in range(1, DT, 2):
                dve.wait_ge(s["turn_ps"], 16 + t + 1)
                dve.tensor_scalar(uT[:, t, :], ps[:, t, 0:TOK], vec[:, V_GMIX2 + t:V_GMIX2 + t + 1], None,
                                  ALU.mult).then_inc(s["turn_dve"], 1)

            for u in range(2 * HEADS + 1):
                if u < 2 * HEADS:
                    hd, i = u // 2, u % 2
                    dve.wait_ge(s["s2_ps"], u + 1)
                    dve.scalar_tensor_tensor(pm2[:, u % 3, :], cst[:, C_DIST + i * TOK:C_DIST + (i + 1) * TOK],
                                             -(2.0 ** (-8.0 * (hd + 1) / HEADS)), ps[:, 2 + u % 2, 0:TOK],
                                             ALU.mult, ALU.add).then_inc(s["s2_sb"], 1)
                    dve.wait_ge(s["s2_sb"], u + 1)
                    link(dve.tensor_reduce(rinv[:, u:u + 1], pm2[:, u % 3, :], AX.X, ALU.max, negate=True))
                    dve.tensor_tensor(nmx[:, u:u + 1], rinv[:, u:u + 1], nsink[:, hd:hd + 1], ALU.min
                                      ).then_inc(s["nm2_done"], 1)
                if u:
                    w = u - 1
                    dve.wait_ge(s["e2_done"], w + 1)
                    link(dve.tensor_tensor(psum_[:, w:w + 1], psum_[:, w:w + 1], esink[:, w:w + 1], ALU.add))
                    link(dve.reciprocal(rinv[:, w:w + 1], psum_[:, w:w + 1]))
                    dve.tensor_scalar(pm2[:, w % 3, :], pm2[:, w % 3, :], rinv[:, w:w + 1], None, ALU.mult
                                      ).then_inc(s["p2_done"], 1)

            for m in range(DT):
                dve.wait_ge(s["sig_done"], m + 1)
                dve.wait_ge(s["br_ps"], m + 1)
                dve.tensor_tensor(gate[:, m, :], gate[:, m, :], ps[:, 2 + m % 4, :], ALU.mult).then_inc(s["br_sb"], 1)
                dve.wait_ge(s["br_sb"], m + 1)
                dve.tensor_tensor(mg[:, m, :], gate[:, m, 0:TOK], gate[:, m, TOK:2 * TOK], ALU.add).then_inc(s["mg_done"], 1)
            dve.wait_ge(s["h3_ps"], 1)
            for i in range(NT):
                for n in range(2):
                    o = h[:, i, n * 512:(n + 1) * 512]
                    last = dve.tensor_tensor(o, o, ps[:, (0, 1, 6, 7)[2 * i + n], :], ALU.add)
                last.then_inc(s["h3_done"], 1)
            for i in range(NT):
                dve.wait_ge(s["rs_done"], 9 + i + 1)
                dve.tensor_scalar(xn2[:, i, :], h[:, i, :], rse[:, i:i + 1], None, ALU.mult).then_inc(s["xn_done"], 1)
            for t in range(1, DT, 2):
                dve.wait_ge(s["turn_ps"], 24 + t + 1)
                dve.tensor_scalar(uT[:, t, :], ps[:, t, 0:TOK], vec[:, V_GFFN2 + t:V_GFFN2 + t + 1], None,
                                  ALU.mult).then_inc(s["turn_dve"], 1)
            for m in range(F2T):
                dve.wait_ge(s["fsg_done"], m + 1)
                dve.tensor_tensor(fh[:, m % 4, :], fsg[:, m % 4, :], ps[:, 4 + m % 4, TOK:2 * TOK], ALU.mult
                                  ).then_inc(s["fh_done"], 1)
            dve.wait_ge(s["facc_ps"], 1)
            for i in range(NT):
                dve.tensor_tensor(h[:, i, :], h[:, i, :], two_banks(2 * i), ALU.add).then_inc(s["h4_done"], 1)
            dve.wait_ge(gain_in, 32)
            for i in range(NT):
                dve.wait_ge(s["rs_done"], 11 + i + 1)
                dve.scalar_tensor_tensor(xn2[:, i, :], h[:, i, :], rsf[:, i:i + 1], gain[:, 0, :], ALU.mult, ALU.mult
                                         ).then_inc(s["y_done"], 1)

        @block.tensor
        def _(pe):
            def mm(o, lhsT, rhs, start, stop, **kw):
                return pe.matmul(o, lhsT, rhs, start=start, stop=stop, **kw)

            def turn(o, a, rows=P):
                return pe.transpose(o, a, ident[0:rows, 0:rows])

            pe.wait_ge(const_in, 48)
            pe.wait_ge(s["xn_done"], 1)
            for t in range(DT):
                turn(ps[:, t, 0:META], xn[0:META, 0, t * P:(t + 1) * P], META)
                turn(ps[:, t, META:META + P], xn[:, 1, t * P:(t + 1) * P])
                turn(ps[:, t, META + P:COLS], xn[:, 2, t * P:(t + 1) * P]).then_inc(s["turn_ps"], 1)

            pe.wait_ge(s["turn_act"], DT // 2)
            pe.wait_ge(s["turn_dve"], DT // 2)
            slot_ready(pe, 0)
            slot_ready(pe, 1)
            for i, m, c in TILES:
                for t in range(DT):
                    last = mm(ps[0:m, i, 0:ZA], xT[:, t, c:c + m],
                              ring[:, t // 4, (t % 4) * ZA:(t % 4 + 1) * ZA], t == 0, t == DT - 1)
                last.then_inc(s["z_ps"], 1)

            for c in range(3 * CT):
                m, kind = c // 3, c % 3
                n = 2 + c // 2
                if c % 2 == 0:
                    slot_ready(pe, n)
                if m == 1 and kind == 2:
                    pe.wait_ge(s["z_sb"], 1)
                if m >= 2 and kind == 0:
                    pe.wait_ge(s["conv_done"], m - 1)
                lo, w = (META, TOK) if kind == 2 else (0, COLS)
                for t in range(DT):
                    last = mm(ps[:, conv_bank(m, kind), 0:w], ring[:, n % SLOTS, (c % 2) * D + t * P:(c % 2) * D + (t + 1) * P],
                              xT[:, t, lo:lo + w], t == 0, t == DT - 1)
                    if t == 0 and c == 0:
                        last.then_inc(used, 2)
                    elif t == 0 and c % 2 == 0:
                        last.then_inc(used, 1)
                last.then_inc(s["conv_ps"], 1)

            pe.wait_ge(s["zn_done"], 1)
            pe.wait_ge(s["z_sb"], 3)
            for f in range(QL // P):
                for i in range(NT):
                    last = turn(ps[:, 1, f * TOK + i * P:f * TOK + (i + 1) * P], zt[:, 1 + i, f * P:(f + 1) * P])
                    if f == 0 and i == 0:
                        last.then_inc(used, 1)
            last.then_inc(s["t3_ps"], 1)
            for i, m, c in TILES:
                last = turn(ps[:, 2, c:c + m], zt[0:m, i, QL:QL + KVL], m)
            last.then_inc(s["t3_ps"], 1)
            pe.wait_ge(s["kr_done"], 1)
            pe.wait_ge(s["conv_done"], CT - 1)
            for i, m, c in TILES:
                last = turn(ps[0:QKD, 3, c:c + m], kr[0:m, i, :], m)
            last.then_inc(s["t3_ps"], 1)

            slot_ready(pe, 9)
            wkv = ring[:, 9 % SLOTS, :]
            pe.wait_ge(s["c_sb"], 3)
            pe.wait_ge(s["conv_done"], CT)
            pe.wait_ge(s["kr_sb"], 1)

            def k_head(hd):
                if hd >= 4:
                    pe.wait_ge(s["kn_sb"], hd - 3)
                mm(ps[0:NOPE, hd % 4, 0:COLS], wkv[:, hd * NOPE:(hd + 1) * NOPE], ckvT, True, True
                   ).then_inc(s["kn_ps"], 1)

            for hd in range(4):
                k_head(hd)
            slot_ready(pe, 8)
            for i in range(NT):
                for b, lo, hi in ((0, 0, 512), (1, 512, HEADS * QKD)):
                    for f in range(QL // P):
                        last = mm(ps[:, 4 + 2 * i + b, 0:hi - lo], cqT[:, f, i * P:(i + 1) * P],
                                  ring[:, 0, f * HEADS * QKD + lo:f * HEADS * QKD + hi], f == 0, f == QL // P - 1)
                last.then_inc(s["q_ps"], 1)
            for hd in range(4, HEADS):
                k_head(hd)
            for i, m in enumerate((P, P, META)):
                pe.wait_ge(s["q_sb"], (1, 1, 2)[i])
                mm(ps[0:m, 4 + i, :], ckvT[:, i * P:i * P + m], wkv[:, HEADS * NOPE:HEADS * (NOPE + VD)], True, True
                   ).then_inc(s["v_ps"], 1)

            pe.wait_ge(s["kn_sb"], HEADS)
            pe.wait_ge(s["qr_done"], NT)
            for hp in range(HEADS // 2):
                for j in range(2):
                    for i in range(NT):
                        last = turn(ps[0:QKD, hp, j * TOK + i * P:j * TOK + (i + 1) * P],
                                    qtok[:, i, (2 * hp + j) * QKD:(2 * hp + j + 1) * QKD])
                        if hp == j == i == 0:
                            last.then_inc(used, 2)
                last.then_inc(s["qt_ps"], 1)

            pe.wait_ge(s["qt_act"], 2)
            pe.wait_ge(s["qt_dve"], 2)
            pe.wait_ge(s["v_sb"], 3)

            def scores(u):
                hd, i = u // 2, u % 2
                nk = META + P if i == 0 else COLS
                if u >= 3:
                    pe.wait_ge(s["s_sb"], u - 2)
                mm(ps[:, u % 3, 0:nk], qT[0:QKD, hd, i * P:(i + 1) * P], kT[0:QKD, hd, 0:nk], True, True
                   ).then_inc(s["s_ps"], 1)

            def key_tiles(i):
                return [(P, 0), (META, P)] if i == 0 else [(P, 0), (P, P), (META, 2 * P)]

            def turn_probs(u):
                pe.wait_ge(s["p_done"], u + 1)
                if u >= 2:
                    pe.wait_ge(s["pt_sb"], u - 1)
                for k, (m, c) in enumerate(key_tiles(u % 2)):
                    last = turn(ps[0:m, 3 + u % 2, k * P:(k + 1) * P], pm1[:, u % 3, c:c + m])
                last.then_inc(s["pt_ps"], 1)

            def values(u):
                hd, i = u // 2, u % 2
                pe.wait_ge(s["pt_sb"], u + 1)
                if hd >= 4 and u % 4 == 0:
                    pe.wait_ge(s["sq_done"], CT + hd // 2 - 1)
                o = ps[(hd % 2) * VD:(hd % 2 + 1) * VD, 6 + (hd // 2) % 2, i * P:(i + 1) * P]
                tiles = key_tiles(i)
                for k, (m, c) in enumerate(tiles):
                    last = mm(o, v1[0:m, k, hd * VD:(hd + 1) * VD], pt1[0:m, u % 2, k * P:(k + 1) * P],
                              k == 0, k == len(tiles) - 1)
                last.then_inc(s["o_ps"], 1)

            scores(0)
            scores(1)
            for u in range(2 * HEADS):
                if u + 2 < 2 * HEADS:
                    scores(u + 2)
                turn_probs(u)
                if u:
                    values(u - 1)
            values(2 * HEADS - 1)

            pe.wait_ge(s["sq_done"], 2 * CT)
            for j in range(2 * NT):
                i, part = j // 2, j % 2
                for m in range(CT):
                    last = mm(ps[:, 5, j:j + 1], sq[:, part * CT + m, i * P:(i + 1) * P], ones[:, 0:1], m == 0, m == CT - 1)
            last.then_inc(s["ssm_ps"], 1)

            pe.wait_ge(s["convg_done"], CT)
            for part in range(2):
                for j in range(2 * NT):
                    i, n = j // 2, j % 2
                    if part == 0 and j == 2:
                        pe.wait_ge(s["msm_done"], 1)
                    for m in range(CT):
                        sl = 10 + 2 * part + m // 2
                        if j == 0 and m % 2 == 0:
                            slot_ready(pe, sl)
                        last = mm(ps[:, 4 * i + 2 * part + n, :], mrg[:, part * CT + m, i * P:(i + 1) * P],
                                  ring[:, sl % SLOTS, (m % 2) * D + n * 512:(m % 2) * D + (n + 1) * 512], m == 0, m == CT - 1)
                        if part == 1 and j == 0 and m == 0:
                            last.then_inc(used, 2)
                    last.then_inc(s["mix_ps"], 1)

            pe.wait_ge(s["mix_done"], 2 * NT)
            pe.wait_ge(s["xn_done"], 1 + NT)
            for t in range(DT):
                for i in range(NT):
                    last = turn(ps[:, t, i * P:(i + 1) * P], xn1[:, i, t * P:(t + 1) * P])
                    if t == 0 and i == 0:
                        last.then_inc(used, 2)
                last.then_inc(s["turn_ps"], 1)

            pe.wait_ge(s["turn_act"], 4 + DT // 2)
            pe.wait_ge(s["turn_dve"], 4 + DT // 2)
            W = GROUPS + EXPERTS
            for i in range(NT):
                for t in range(DT):
                    last = mm(ps[:, 6, i * W:(i + 1) * W], tT[:, t, i * P:(i + 1) * P],
                              vec[:, V_ROUTE + t * W:V_ROUTE + (t + 1) * W], t == 0, t == DT - 1)
            last.then_inc(s["lg_ps"], 1)
            slot_ready(pe, 14)
            slot_ready(pe, 15)
            for f in range(2):
                for b in range(2):
                    for t in range(DT):
                        last = mm(ps[:, 4 + f, b * TOK:(b + 1) * TOK], ring[:, (14 + b) % SLOTS, t * FF + f * P:t * FF + (f + 1) * P],
                                  tT[:, t, :], t == 0, t == DT - 1)
                last.then_inc(s["sgu_ps"], 1)
            pe.wait_ge(s["chosen_done"], 1)
            E = EXPERTS
            mm(ps[:, 7, 0:E], tri, chosen[:, 0, :], True, True).then_inc(used, 2)
            mm(ps[:, 7, E:2 * E], ones, chosen[:, 0, :], True, False)
            mm(ps[:, 7, E:2 * E], tri, chosen[:, 1, :], False, True)
            mm(ps[:, 7, 2 * E:3 * E], ones, chosen[:, 0, :], True, False)
            mm(ps[:, 7, 2 * E:3 * E], ones, chosen[:, 1, :], False, True).then_inc(s["rank_ps"], 1)
            pe.wait_ge(s["hs_done"], 2)
            slot_ready(pe, 16)
            for i in range(NT):
                for n in range(2):
                    for f in range(2):
                        last = mm(ps[:, 2 * i + n, :], hs[:, f, i * P:(i + 1) * P],
                                  ring[:, 16 % SLOTS, f * D + n * 512:f * D + (n + 1) * 512], f == 0, False,
                                  skip_group_check=True)
            last.then_inc(used, 1)

            pe.wait_ge(s["xl_done"], NT)
            pe.wait_ge(s["rounds_done"], 1)
            rounds = pe.value_load(rounds_i[0:1, 0:1], min_val=1, max_val=GROUPS)
            with pe.Fori(0, rounds) as r:
                with pe.Fori(0, GROUPS) as g:
                    it = pe.snap(r * GROUPS + g)

                    def moe_slot(k):
                        n = B1 + k
                        pe.wait_ge(full[n % SLOTS], it * (16 * MOE_GROUP // SLOTS) + 16 * (n // SLOTS + 1))
                        return ring[:, n % SLOTS, :]

                    pe.wait_ge(s["sel_done"], it + 1)
                    for p in range(PAIRS):
                        for i in range(NT):
                            last = turn(ps[:, 4 + p // 2, (p % 2) * TOK + i * P:(p % 2) * TOK + (i + 1) * P],
                                        sel[:, i, p * P:(p + 1) * P].bitcast(F32))
                        if p % 2:
                            last.then_inc(s["st_ps"], 1)
                    for p in range(PAIRS):
                        for i in range(NT):
                            last = mm(ps[:, 6, 2 * p:2 * p + 2], sel[:, i, p * P:(p + 1) * P].bitcast(F32),
                                      comb[:, i, bass.ds(g * PER_GROUP + 2 * p, 2)], i == 0, i == NT - 1)
                    last.then_inc(s["st_ps"], 1)
                    for t in range(DT):
                        if 1 <= t < 4:
                            pe.wait_ge(s["st_sb"], it * 3 + t)
                        elif t >= 4 and t % 2 == 0:
                            pe.wait_ge(s["xg_act"], it * (DT // 2) + (t - 4) // 2 + 1)
                        elif t >= 4:
                            pe.wait_ge(s["xg_dve"], it * (DT // 2) + (t - 5) // 2 + 1)
                        for k, (a, i) in enumerate(((xh, 0), (xh, 1), (xl, 0), (xl, 1))):
                            last = mm(ps[:, gather_bank(t), :], a[:, i, t * P:(t + 1) * P], sel[:, i, :], k == 0, k == 3)
                        last.then_inc(s["xg_ps"], 1)
                    pe.wait_ge(s["xg_act"], it * (DT // 2) + DT // 2)
                    pe.wait_ge(s["xg_dve"], it * (DT // 2) + DT // 2)

                    def gate_up(p):
                        k0 = 4 * p if p < 2 else 6 * p - 2
                        for b in range(2):
                            w = [moe_slot(k0 + 2 * b), moe_slot(k0 + 2 * b + 1)]
                            for t in range(DT):
                                for e in range(2):
                                    last = mm(ps[e * CAP:(e + 1) * CAP, 4 + p % 2, b * FF:(b + 1) * FF],
                                              xg[:, t, (2 * p + e) * CAP:(2 * p + e + 1) * CAP],
                                              w[e][:, t * FF:(t + 1) * FF], t == 0, t == DT - 1)
                                    if t == e == 0 and b:
                                        last.then_inc(used, 2)
                        last.then_inc(s["gu_ps"], 1)

                    def turn_hidden(p):
                        pe.wait_ge(s["ht_done"], it * PAIRS + (p + 1))
                        for j in range(FF // P):
                            last = turn(ps[:, 4 + p % 2, j * P:(j + 1) * P], htok[:, j * P:(j + 1) * P])
                            if j == 0:
                                last.then_inc(used, 2)
                        last.then_inc(s["ht_ps"], 1)

                    def down(p, frees):
                        k0 = (8, 14, 20, 22)[p]
                        w = [moe_slot(k0), moe_slot(k0 + 1)]
                        pe.wait_ge(s["hid_done"], it * PAIRS + (p + 1))
                        for n in range(2):
                            for j in range(FF // P):
                                for e in range(2):
                                    last = mm(ps[e * CAP:(e + 1) * CAP, 6 + n, :], hid[:, j, e * CAP:(e + 1) * CAP],
                                              w[e][:, j * D + n * 512:j * D + (n + 1) * 512], j == 0, j == 1)
                                    if n == j == e == 0 and frees:
                                        last.then_inc(used, frees)
                            last.then_inc(s["y_ps"], 1)

                    def scatter(p, frees):
                        pe.wait_ge(s["yl_done"], it * (2 * PAIRS) + 2 * p + 2)
                        for q in range(2 * NT):
                            i, n = q // 2, q % 2
                            for k, y in enumerate((yh, yl)):
                                last = mm(ps[:, 2 * i + n, :], selT[:, p, i * P:(i + 1) * P], y[:, n * 512:(n + 1) * 512],
                                          False, False, skip_group_check=True)
                                if q == 0 and k == 0 and frees:
                                    last.then_inc(used, frees)
                        return last

                    for p in range(PAIRS):
                        gate_up(p)
                        if p >= 2:
                            scatter(p - 2, 2)
                        if p:
                            down(p - 1, 2 if p == 1 else 0)
                        turn_hidden(p)
                    scatter(PAIRS - 2, 0)
                    down(PAIRS - 1, 0)
                    scatter(PAIRS - 1, 2).then_inc(s["moe_done"], 1)

            pe.wait_ge(s["xn_done"], 3 + NT)
            for t in range(DT):
                for i in range(NT):
                    last = turn(ps[:, t, i * P:(i + 1) * P], xn2[:, i, t * P:(t + 1) * P])
                last.then_inc(s["turn_ps"], 1)
            pe.wait_ge(s["turn_act"], 8 + DT // 2)
            pe.wait_ge(s["turn_dve"], 8 + DT // 2)

            def chunk(o, n, half, frees=0, rhs=None):
                for t in range(DT):
                    last = mm(o, ring[:, place2(n), half * D + t * P:half * D + (t + 1) * P], uT[:, t, :], t == 0, t == DT - 1)
                    if t == 0 and frees:
                        last.then_inc(used2, frees)
                return last

            for c in range(4):
                if c % 2 == 0:
                    slot2_ready(pe, c // 2)
                chunk(ps[:, c, 0:TOK], c // 2, c % 2, frees=1 if c == 2 else 0).then_inc(s["z2_ps"], 1)
            for c in range(CT):
                if c % 2 == 0:
                    slot2_ready(pe, 2 + c // 2)
                chunk(ps[:, 4 + c, 0:TOK], 2 + c // 2, c % 2, frees=1 - c % 2).then_inc(s["q2_ps"], 1)
            slot2_ready(pe, 4)
            for c in range(2):
                pe.wait_ge(s["z2_sb"], c + 1)
                chunk(ps[:, c, 0:TOK], 4, c, frees=1 - c).then_inc(s["k2_ps"], 1)
            slot2_ready(pe, 5)
            pe.wait_ge(s["z2_sb"], 3)
            for i in range(NT):
                for t in range(DT):
                    last = mm(ps[:, 2, i * P:(i + 1) * P], uT[:, t, i * P:(i + 1) * P],
                              ring[:, place2(5), t * P:(t + 1) * P], t == 0, t == DT - 1)
                    if t == i == 0:
                        last.then_inc(used2, 1)
            last.then_inc(s["v2_ps"], 1)
            pe.wait_ge(s["v2_sb"], 1)
            pe.wait_ge(s["q2_sb"], CT)
            pe.wait_ge(s["k2_sb"], 2)

            def scores2(u):
                hd, i = u // 2, u % 2
                lo = (hd % 2) * HD
                if u >= 2:
                    pe.wait_ge(s["s2_sb"], u - 1)
                mm(ps[:, 2 + u % 2, 0:TOK], q2T[lo:lo + HD, hd // 2, i * P:(i + 1) * P], k2T[lo:lo + HD, hd // 4, :],
                   True, True).then_inc(s["s2_ps"], 1)

            def turn_probs2(u):
                pe.wait_ge(s["p2_done"], u + 1)
                if u >= 2:
                    pe.wait_ge(s["pt2_sb"], u - 1)
                for k in range(NT):
                    last = turn(ps[:, 4 + u % 2, k * P:(k + 1) * P], pm2[:, u % 3, k * P:(k + 1) * P])
                last.then_inc(s["pt2_ps"], 1)

            def values2(u):
                hd, i = u // 2, u % 2
                kv = hd // 4
                pe.wait_ge(s["pt2_sb"], u + 1)
                if hd >= 4 and u % 4 == 0:
                    pe.wait_ge(s["o2_sb"], hd // 2 - 1)
                o = ps[(hd % 2) * HD:(hd % 2 + 1) * HD, 6 + (hd // 2) % 2, i * P:(i + 1) * P]
                for k in range(NT):
                    last = mm(o, v2[:, k, kv * HD:(kv + 1) * HD], pt2[:, u % 2, k * P:(k + 1) * P], k == 0, k == NT - 1)
                last.then_inc(s["o2_ps"], 1)

            scores2(0)
            for u in range(2 * HEADS):
                m = u // 2
                if u % 2 == 0:
                    slot2_ready(pe, 6 + m)
                    if m >= 2:
                        pe.wait_ge(s["g_sb"], m - 1)
                last = chunk(ps[:, m % 2, (u % 2) * TOK:(u % 2 + 1) * TOK], 6 + m, u % 2, frees=1 - u % 2)
                if u % 2:
                    last.then_inc(s["g_ps"], 1)
                if u + 1 < 2 * HEADS:
                    scores2(u + 1)
                turn_probs2(u)
                if u:
                    values2(u - 1)
            values2(2 * HEADS - 1)

            for c in range(4):
                pe.wait_ge(s["dp_done"], c + 1)
                if c < 2:
                    pe.wait_ge(s["g_sb"], DT)
                else:
                    pe.wait_ge(s["yp_sb"], c - 1)
                mm(ps[:, c % 2, 0:TOK], vec[:, V_PG + c * P:V_PG + (c + 1) * P], dp[:, c, :], True, True
                   ).then_inc(s["yp_ps"], 1)
            for k in range(14, 18):
                slot2_ready(pe, k)
            pe.wait_ge(s["yp_sb"], 4)
            pe.wait_ge(s["o2_sb"], CT)
            for m in range(DT):
                if m >= 4:
                    pe.wait_ge(s["br_sb"], m - 3)
                for b, src in ((0, yp), (1, at2)):
                    for k in range(4):
                        last = mm(ps[:, 2 + m % 4, b * TOK:(b + 1) * TOK],
                                  ring[:, place2(14 + 2 * b + k // 2), (k % 2) * D + m * P:(k % 2) * D + (m + 1) * P],
                                  src[:, k, :], k == 0, k == 3)
                        if m == b == k == 0:
                            last.then_inc(used2, 1)
                last.then_inc(s["br_ps"], 1)
            pe.wait_ge(s["mg_done"], DT)
            for k in range(DT):
                if k % 2 == 0:
                    slot2_ready(pe, 18 + k // 2)
                for q in range(2 * NT):
                    i, n = q // 2, q % 2
                    last = mm(ps[:, (0, 1, 6, 7)[q], :], mg[:, k, i * P:(i + 1) * P],
                              ring[:, place2(18 + k // 2), (k % 2) * D + n * 512:(k % 2) * D + (n + 1) * 512],
                              k == 0, k == DT - 1, skip_group_check=True)
                    if k == 0 and q == 0:
                        last.then_inc(used2, 4)
                    elif k % 2 == 0 and q == 0:
                        last.then_inc(used2, 1)
            last.then_inc(s["h3_ps"], 1)

            pe.wait_ge(s["h3_done"], NT)
            pe.wait_ge(s["mg_done"], DT)
            pe.wait_ge(s["xn_done"], 5 + NT)
            for t in range(DT):
                for i in range(NT):
                    last = turn(ps[:, t, i * P:(i + 1) * P], xn2[:, i, t * P:(t + 1) * P])
                    if t == i == 0:
                        last.then_inc(used2, 1)
                last.then_inc(s["turn_ps"], 1)
            pe.wait_ge(s["turn_act"], 12 + DT // 2)
            pe.wait_ge(s["turn_dve"], 12 + DT // 2)

            def ffn_gate_up(m):
                n = B2 + m if m < 2 else B2 + 2 + 3 * ((m - 2) // 2) + m % 2
                slot2_ready(pe, n)
                if m >= 4:
                    pe.wait_ge(s["fh_done"], m - 3)
                for b in range(2):
                    for t in range(DT):
                        last = mm(ps[:, 4 + m % 4, b * TOK:(b + 1) * TOK], ring[:, place2(n), b * D + t * P:b * D + (t + 1) * P],
                                  uT[:, t, :], t == 0, t == DT - 1)
                        if b == t == 0 and m:
                            last.then_inc(used2, 1)
                last.then_inc(s["f_ps"], 1)

            def ffn_down(i2):
                n = B2 + 2 + 3 * i2 + (2 if i2 < F2T // 2 - 1 else 0)
                slot2_ready(pe, n)
                pe.wait_ge(s["fh_done"], 2 * i2 + 2)
                for m in (2 * i2, 2 * i2 + 1):
                    for q in range(2 * NT):
                        i, nn = q // 2, q % 2
                        last = mm(ps[:, q, :], fh[:, m % 4, i * P:(i + 1) * P],
                                  ring[:, place2(n), (m % 2) * D + nn * 512:(m % 2) * D + (nn + 1) * 512],
                                  m == 0, m == F2T - 1, skip_group_check=True)
                        if m % 2 == 0 and q == 0:
                            last.then_inc(used2, 1)
                return last

            ffn_gate_up(0)
            ffn_gate_up(1)
            for i2 in range(F2T // 2):
                if i2 < F2T // 2 - 1:
                    ffn_gate_up(2 * i2 + 2)
                    ffn_gate_up(2 * i2 + 3)
                last = ffn_down(i2)
            last.then_inc(s["facc_ps"], 1)


def shape_constants():
    import numpy as np
    c = np.zeros((P, CN), np.float32)
    c[:, C_ID:C_ID + P] = np.eye(P)
    q = np.arange(P)[:, None]
    k = np.arange(P)[None, :]
    c[:, C_MASK + COLS - P:C_MASK + COLS] = np.where(k <= q, 0.0, -BIG)
    c[:, C_TRI:C_TRI + P] = q < k
    c[:, C_ONE:C_ONE + P] = 1.0
    c[:, C_IOTA:C_IOTA + CAP] = np.arange(CAP)
    c[:, C_DESC:C_DESC + EXPERTS] = EXPERTS - np.arange(EXPERTS)
    for i in range(NT):
        dist = np.abs(q + i * P - np.arange(TOK)[None, :]).astype(np.float32)
        c[:, C_DIST + i * TOK:C_DIST + (i + 1) * TOK] = np.where(dist <= 128, dist, 1e34)
    t = np.arange(TOK)
    for g, w in enumerate(POOL_WINDOWS):
        n = np.clip(t + w // 2, 0, TOK) - np.clip(t - w // 2, 0, TOK)
        c[:, C_CNT + g * TOK:C_CNT + (g + 1) * TOK] = 1.0 / n
    f = np.float32(1.0) / (np.float32(10000.0) ** (np.arange(0, ROPE, 2, dtype=np.float32) / np.float32(ROPE)))
    c[:, C_FREQ:C_FREQ + ROPE // 2] = f
    c[0:META, C_POS] = np.arange(META)
    c[:, C_NHALF] = -0.5
    return c


def packed(inputs):
    import numpy as np

    def per_partition(name, i0=0):
        a = np.asarray(inputs[name])[i0].reshape(-1, P)
        return a.T

    def over(a):
        return np.broadcast_to(np.asarray(a).reshape(1, -1), (P, np.asarray(a).size))

    conv = np.asarray(inputs["conv_w"])[0].reshape(3 * CT, P).T
    route = np.concatenate([np.asarray(inputs["w_group_router"])[0], np.asarray(inputs["w_expert_router"])[0]], 1)
    route = route.reshape(DT, P, -1).transpose(1, 0, 2).reshape(P, -1)
    maps = np.asarray(inputs["w_pool_group_2"])[0].transpose(1, 0, 2).reshape(P, -1)
    small = np.concatenate([
        per_partition("pre_mix_norm"), per_partition("q_norm"), per_partition("kv_norm"), conv,
        per_partition("attn_out_norm"), per_partition("conv_out_norm"), per_partition("pre_ffn_norm"),
        per_partition("norm_mix_2"), per_partition("norm_ffn_2"), per_partition("pool_scale_2"),
        over(inputs["b_group_router"]), over(inputs["b_expert_router"]), over(inputs["sink_2"]), route, maps], 1)
    assert small.shape == (P, VN)
    gains = np.stack([over(inputs[n]) for n in ("post_mix_norm", "post_ffn_norm", "norm_final_2")], 1)
    return np.ascontiguousarray(small), np.ascontiguousarray(gains)


def weight_stream(inputs):
    import numpy as np
    w = {k: np.asarray(inputs[k])[0] for k in (
        "w_in", "w_uq", "w_ukv", "w_out", "w_sh_gate", "w_sh_up", "w_sh_down", "w_gate", "w_up", "w_down", "w_in_2",
        "w_pool_branch_2", "w_attn_branch_2", "w_out_2", "w_ffn_gate_2", "w_ffn_up_2", "w_ffn_down_2")}
    out = np.zeros((STREAM, P, SLOT), np.float32)
    at = [0]

    def put(*parts):
        c = 0
        for a in parts:
            a = a.reshape(a.shape[0] // P, P, a.shape[1]).transpose(1, 0, 2).reshape(P, -1)
            out[at[0], :, c:c + a.shape[1]] = a
            c += a.shape[1]
        at[0] += 1

    def cols(a, lo, n=P):
        return a[:, lo:lo + n]

    wi = w["w_in"]
    put(wi[0:D // 2, 0:ZA])
    put(wi[D // 2:D, 0:ZA])
    gb, gc, xi = ZA, ZA + 512, ZA + 1024
    chunks = [cols(wi, base + m * P) for m in range(CT) for base in (gc, xi, gb)]
    for c in range(0, len(chunks), 2):
        put(chunks[c], chunks[c + 1])
    put(w["w_uq"])
    kv = w["w_ukv"].reshape(KVL, HEADS, NOPE + VD)
    put(kv[:, :, 0:NOPE].reshape(KVL, -1), kv[:, :, NOPE:].reshape(KVL, -1))
    for k in range(4):
        put(w["w_out"][k * 256:(k + 1) * 256])
    put(w["w_sh_gate"])
    put(w["w_sh_up"])
    put(w["w_sh_down"])
    for e in range(0, EXPERTS, 2):
        pair = (e // 2) % PAIRS
        for name in ("w_gate", "w_up"):
            put(w[name][e])
            put(w[name][e + 1])
        for back in ((), (2,), (2,), (2, 0))[pair]:
            put(w["w_down"][e - back])
            put(w["w_down"][e - back + 1])
    w2 = w["w_in_2"]
    q0, k0, v0, gp0, ga0 = 512, 1024, 1152, 1280, 2304
    for c in range(0, 4, 2):
        put(cols(w2, c * P), cols(w2, (c + 1) * P))
    for c in range(0, 4, 2):
        put(cols(w2, q0 + c * P), cols(w2, q0 + (c + 1) * P))
    ka, kb = cols(w2, k0, HD), cols(w2, k0 + HD, HD)
    put(np.concatenate([ka, ka], 1), np.concatenate([kb, kb], 1))
    put(cols(w2, v0))
    for m in range(DT):
        put(cols(w2, gp0 + m * P), cols(w2, ga0 + m * P))
    for name, n in (("w_pool_branch_2", 2), ("w_attn_branch_2", 2), ("w_out_2", 4)):
        for k in range(n):
            put(w[name][k * 256:(k + 1) * 256])
    gate, up, down = w["w_ffn_gate_2"], w["w_ffn_up_2"], w["w_ffn_down_2"]
    for m in (0, 1):
        put(cols(gate, m * P), cols(up, m * P))
    for i in range(F2T // 2):
        if i < F2T // 2 - 1:
            for m in (2 * i + 2, 2 * i + 3):
                put(cols(gate, m * P), cols(up, m * P))
        put(down[i * 256:(i + 1) * 256])
    assert at[0] == STREAM, (at[0], STREAM)
    return out


def kernel(**inputs):
    import numpy as np
    import concourse.bacc as bacc
    from concourse.bass_utils import run_bass_kernel_spmd

    small, gains = packed(inputs)
    arrays = {
        "x": np.ascontiguousarray(np.asarray(inputs["x"])[0]),
        "meta": np.ascontiguousarray(np.asarray(inputs["meta_tokens"])),
        "consts": shape_constants(),
        "small": small,
        "gains": gains,
        "positions": np.ascontiguousarray(np.asarray(inputs["positions"])[0].reshape(NT, P).T),
        "stream": weight_stream(inputs),
    }
    nc = bacc.Bacc("TRN2", target_bir_lowering=False, num_devices=1)
    args = [nc.dram_tensor(f"{n}_dram", a.shape, mybir.dt.from_np(a.dtype), kind="ExternalInput").ap()
            for n, a in arrays.items()]
    out = nc.dram_tensor("out_dram", (TOK, D), F32, kind="ExternalOutput").ap()
    two_blocks(nc, *args, out)
    r = run_bass_kernel_spmd(nc, [{f"{n}_dram": a for n, a in arrays.items()}], core_ids=[0])
    return r.results[0]["out_dram"].reshape(1, TOK, D)
```

```python
from contextlib import ExitStack

import concourse.bass as bass
from concourse import mybir

F32 = mybir.dt.float32
F32R = mybir.dt.float32r
I32 = mybir.dt.int32
ALU = mybir.AluOpType
ACT = mybir.ActivationFunctionType
AX = mybir.AxisListType

P = 128
D = 1024
DT = D // P
TOK = 256
NT = TOK // P
META = 16
COLS = META + TOK
EPS = 1e-6
BIG = 1e30

HEADS = 8
NOPE, ROPE, VD = 64, 32, 64
QKD = NOPE + ROPE
QL, KVL = 256, 128
ZA = QL + KVL + ROPE
CT = 512 // P
ATTN_SCALE = QKD ** -0.5
FILL = 3

GROUPS, PER_GROUP, EXPERTS, FF = 4, 8, 32, 256
CAP = 64
PAIRS = PER_GROUP // 2

POOL_WINDOWS = (2, 4, 8, 16)
PAD = 8
HD = 64
FF2 = 2816
F2T = FF2 // P

SLOTS = 8
SLOT = 2048
WORK = 17408
B1 = 17
Q_SLOT = 8
SPLIT1 = 12
MOE_GROUP = 3 * PER_GROUP
B2 = 22
FFN_SLOTS = 3 * F2T // 2
STREAM = B1 + GROUPS * MOE_GROUP + B2 + FFN_SLOTS

C_ID = 0
C_FREQ = C_ID + P
C_POS = C_FREQ + ROPE // 2
C_NHALF = C_POS + 1
C_FIRST = C_NHALF + 1
C_MASK = C_FIRST
C_TRI = C_MASK + COLS
C_ONE = C_TRI + P
C_IOTA = C_ONE + P
C_DESC = C_IOTA + CAP
C_DIST = C_DESC + EXPERTS
C_CNT = C_DIST + NT * TOK
CN = C_CNT + 4 * TOK

V_GMIX = 0
V_GQ = V_GMIX + DT
V_GKV = V_GQ + QL // P
V_CONV = V_GKV + 1
V_GATT = V_CONV + 3 * CT
V_GCONV = V_GATT + CT
V_GFFN = V_GCONV + CT
V_GMIX2 = V_GFFN + DT
V_GFFN2 = V_GMIX2 + DT
V_PSC = V_GFFN2 + DT
V_RB = V_PSC + 4
V_SINK = V_RB + GROUPS + EXPERTS
V_ROUTE = V_SINK + HEADS
V_PG = V_ROUTE + DT * (GROUPS + EXPERTS)
VN = V_PG + 4 * P

TWO_PI = 6.283185307179586
PI_1 = 6.28125
PI_2 = 0.0019350051879882812
PI_3 = TWO_PI - PI_1 - PI_2
ROUND_MAGIC = 12582912.0
PI_F32 = 3.1415925


def two_blocks(nc, x, meta, consts, small, gains, positions, stream, out):
    ctx = ExitStack()
    with ctx:
        def sb(name, shape, dt=F32):
            return ctx.enter_context(nc.sbuf_tensor(name, shape, dt))

        def sem(name):
            return ctx.enter_context(nc.semaphore(name))

        ring = sb("ring", [P, SLOTS, SLOT])
        h = sb("h", [P, NT, D])
        cst = sb("cst", [P, CN])
        vec = sb("vec", [P, VN])
        gain = sb("gain", [P, D])
        stat = sb("stat", [P, 160])
        pos_i = sb("pos_i", [P, NT], I32)
        rounds_i = sb("rounds_i", [P, 1], I32)

        single = sb("single", [P, 4 * SLOT], F32R)
        turned = sb("turned", [P, 2, DT * COLS], F32R)

        def halved(a, n, w):
            return a[:, 0:n * w].rearrange("p (a b) -> p a b", b=w)

        xh = halved(single, NT, D)
        xl = halved(single[:, NT * D:2 * NT * D], NT, D)
        sel = halved(single[:, 2 * SLOT:], NT, PER_GROUP * CAP)
        selT = halved(single[:, 5 * SLOT // 2:], PAIRS, TOK)
        yh = single[:, 3 * SLOT:3 * SLOT + D]
        yl = single[:, 3 * SLOT + D:4 * SLOT]
        w_hi = [single[:, 0:SLOT], single[:, 2 * SLOT:3 * SLOT]]
        w_lo = [single[:, SLOT:2 * SLOT], single[:, 3 * SLOT:4 * SLOT]]

        work_at = -(-nc.sbuf_base // 512) * 512
        work = nc.alloc_sbuf_tensor_at("work", [P, WORK], F32, offset=work_at)
        work_r = nc.alloc_sbuf_tensor_at("work_r", [P, WORK], F32R, offset=work_at)
        top = [0]

        def cut(*shape, dt=F32):
            n = 1
            for s in shape:
                n *= s
            a = (work if dt is F32 else work_r)[:, top[0]:top[0] + n]
            top[0] += n
            assert top[0] <= WORK, top
            if len(shape) == 2:
                return a.rearrange("p (a b) -> p a b", b=shape[1])
            return a

        ps = ctx.enter_context(nc.psum_tensor("ps", [P, 8, 512], F32))

        ident = cst[:, C_ID:C_ID + P]
        ones = cst[:, C_ONE:C_ONE + P]
        tri = cst[:, C_TRI:C_TRI + P]
        mask = cst[:, C_MASK:C_MASK + COLS]

        def scol(n):
            a = top_stat[0]
            top_stat[0] += n
            return stat[:, a:a + n]
        top_stat = [0]

        xn = cut(NT + 1, D)
        zt_at = top[0]
        zt = cut(NT + 1, ZA)
        kr = cut(NT + 1, QKD)
        tabs = cut(8, 3 * ROPE // 2)
        cqT = cut(QL // P, TOK)
        ckvT = cut(COLS)
        cmix = cut(2 * NT, 512)
        qtok = cut(NT, HEADS * QKD)
        qT = cut(HEADS, TOK)
        kT = cut(HEADS, COLS)
        v1 = cut(NT + 1, HEADS * VD)
        mrg = cut(CT, TOK)
        sq = xn.rearrange("p a b -> p (a b)")[:, 0:2 * CT * TOK].rearrange("p (a b) -> p a b", b=TOK)
        rt = cut(4, HEADS * ROPE // 2)
        meta_raw = mrg.rearrange("p a b -> p (a b)")[0:META, 0:D]
        x_hi, x_lo = (halved(turned[:, j, :], DT, COLS) for j in range(2))
        mrg_hi, mrg_lo = (halved(turned[:, j, :], DT, TOK) for j in range(2))
        gct = qtok.rearrange("p a b -> p (a b)")[:, 0:2 * COLS].rearrange("p (a b) -> p a b", b=COLS)
        u_t = qT.rearrange("p a b -> p (a b)")[:, 0:COLS]
        cy = qT.rearrange("p a b -> p (a b)")[:, COLS:COLS + TOK]
        pm1 = work[:, zt_at:zt_at + 3 * COLS].rearrange("p (a b) -> p a b", b=COLS)
        pt1 = work[:, zt_at + 3 * COLS:zt_at + 3 * COLS + 2 * 384].rearrange("p (a b) -> p a b", b=384)
        gmix = cmix.rearrange("p a b -> p (a b)").rearrange("p (a b) -> p a b", b=D)
        mix = qT.rearrange("p a b -> p (a b)").rearrange("p (a b) -> p a b", b=D)
        top[0] = 0

        xn1 = cut(NT, D)
        tT = cut(DT, TOK)
        xg = cut(DT, PER_GROUP * CAP)
        mixb = cut(NT, D)
        sg_s = cut(2, TOK)
        hs = cut(2, TOK)
        sg = cut(FF)
        htok = cut(FF)
        hid = cut(FF // P, P)
        route = cut(24, NT * EXPERTS)
        logT = cut(TOK)
        logit = cut(NT, GROUPS + EXPERTS)
        rankp = cut(NT, EXPERTS + PER_GROUP)
        comb = cut(NT, EXPERTS)
        chosen = cut(NT, EXPERTS)
        wsl = cut(PAIRS)
        cnt = cut(EXPERTS)
        squares = [xg[:, 0:2, :], xg[:, 2:4, :]]
        top[0] = 0

        xn2 = cut(NT, D)
        zp = cut(4, TOK + 2 * PAD)
        win = cut(2, TOK + 2 * PAD)
        dp = cut(4, TOK)
        yp_hi, yp_lo = cut(4, TOK, dt=F32R), cut(4, TOK, dt=F32R)
        q2T = cut(CT, TOK)
        k2T = cut(2, TOK)
        v2 = cut(NT, P)
        gate_at = top[0]
        gate = cut(DT, 2 * TOK)
        at_hi, at_lo = cut(CT, TOK, dt=F32R), cut(CT, TOK, dt=F32R)
        pm2 = cut(3, TOK)
        pt2 = cut(2, TOK)
        u_hi, u_lo = (turned[:, j, 0:DT * TOK].rearrange("p (a b) -> p a b", b=TOK) for j in range(2))
        mg_hi, mg_lo = u_hi, u_lo
        top[0] = gate_at
        fsg, fh = cut(4, TOK), cut(4, TOK)
        fh_hi, fh_lo = cut(4, TOK, dt=F32R), cut(4, TOK, dt=F32R)

        ssx, msx, rsx = scol(3), scol(3), scol(3)
        ssz, msz, rsz = scol(5), scol(5), scol(5)
        nmx, psum_, rinv = scol(16), scol(16), scol(16)
        msm, rsm = scol(4), scol(4)
        ssa, msa, rsa = scol(2), scol(2), scol(2)
        ssb, msb, rsb = scol(2), scol(2), scol(2)
        ssc, msc, rsc = scol(2), scol(2), scol(2)
        ssd, msd, rsd = scol(2), scol(2), scol(2)
        sse, mse, rse = scol(2), scol(2), scol(2)
        ssf, msf, rsf = scol(2), scol(2), scol(2)
        nsink = scol(HEADS)
        esink = scol(16)
        posf = scol(3)

        x_in, x1_in, out_st = sem("x_in"), sem("x1_in"), sem("out_st")
        const_in, const2_in, gain_in = sem("const_in"), sem("const2_in"), sem("gain_in")
        full = [sem(f"slot_full{i}") for i in range(SLOTS)]
        full2 = [sem(f"slot2_full{i}") for i in range(SLOTS)]
        used, split_used = sem("slots_used"), sem("split_used")
        names = """init ss_done rs_done xn_done turn_ps turn_act turn_dve z_ps z_sb rz_done zn_done kr_done
            conv_ps gc_sb conv_done convg_done t3_ps c_sb kr_sb q_ps q_sb kn_ps kn_sb v_ps v_sb qr_done
            qt_ps qt_act qt_dve s_ps s_sb nm_done e_done p_done pt_ps pt_sb o_ps sq_done ssm_ps msm_done
            rsm_done mix_ps mix_done h1_done xh_done xl_done lt_ps lt_sb lg_ps route_a route_b route_c route_d
            chosen_done rank_ps rounds_done sgu_ps ssg_done hs_done cms_done gmix_done gmoe_done dve_step pool_step sin_in tab_done
            sel_done rank_step st_ps st_sb xg_ps xg_act xg_dve gu_ps sg_done ht_done ht_ps hid_done y_ps yh_done yl_done
            moe_done h2_done z2_ps z2_sb q2_ps q2_sb k2_ps k2_sb v2_ps v2_sb g_ps g_sb zpad_done dp_done
            yp_ps yp_sb s2_ps s2_sb nm2_done e2_done p2_done pt2_ps pt2_sb o2_ps o2_sb sig_done br_ps br_sb
            mg_done h3_ps h3_done f_ps fsg_done fh_sum fh_high fh_done facc_ps whi_done wlo_done o2_low yp_low mg_sum mg_high att_low cm_ps cm_sb sqs_done h4_done y_done""".split()
        s = {n: sem(n) for n in names}

        def slot_ready(eng, n):
            eng.wait_ge(full[n % SLOTS], 16 * (n // SLOTS + 1))

        def slot2_ready(eng, n):
            eng.wait_ge(full2[n % SLOTS], 16 * (n // SLOTS + 1))

        early_splits, late_splits = ((4,), (5,), (7,), ()), ((), (6,), (), ())

        def split_slot(k):
            if k < SPLIT1:
                n = k if k < Q_SLOT else k + 2
                return n % SLOTS, full[n % SLOTS], 16 * (n // SLOTS + 1)
            n = k - SPLIT1
            return place2(n), full2[n % SLOTS], 16 * (n // SLOTS + 1)

        def split_high(act, k):
            for half in range(2):
                split_high_half(act, k, half)

        def split_high_half(act, k, half):
            place, came, count = split_slot(k)
            if half == 0:
                if k >= 2:
                    act.wait_ge(split_used, k - 1)
                act.wait_ge(came, count)
            a = slice(half * D, (half + 1) * D)
            act.activation(w_hi[k % 2][:, a], ring[:, place, a], ACT.Copy).then_inc(s["whi_done"], 1)

        def split_low_half(dve, k, half):
            dve.wait_ge(s["whi_done"], 2 * k + half + 1)
            a = slice(half * D, (half + 1) * D)
            dve.tensor_tensor(w_lo[k % 2][:, a], ring[:, split_slot(k)[0], a], w_hi[k % 2][:, a].bitcast(F32), ALU.subtract
                              ).then_inc(s["wlo_done"], 1)

        def split_low(dve, k):
            for half in range(2):
                split_low_half(dve, k, half)

        def place2(n):
            return (B1 + GROUPS * MOE_GROUP + n) % SLOTS

        def two_banks(b):
            return ps[:, b:b + 2, :].rearrange("p a b -> p (a b)")

        def conv_bank(m, kind):
            return ((3, 4, 5), (6, 7, 0))[m % 2][kind]

        def gather_bank(t):
            return (7, 4, 5, 6)[t % 4]

        def attention_out(act, hp):
            act.wait_ge(s["o_ps"], 4 * (hp + 1))
            act.activation(mrg_hi[:, hp, :], ps[:, 6 + hp % 2, 0:TOK], ACT.Copy, scale=vec[:, V_GATT + hp:V_GATT + hp + 1])
            act.activation(sq[:, hp, :], ps[:, 6 + hp % 2, 0:TOK], ACT.Square).then_inc(s["sq_done"], 1)

        def attention_low(dve, hp):
            dve.wait_ge(s["sq_done"], CT + hp + 1)
            dve.scalar_tensor_tensor(mrg_lo[:, hp, :], ps[:, 6 + hp % 2, 0:TOK], vec[:, V_GATT + hp:V_GATT + hp + 1],
                                     mrg_hi[:, hp, :].bitcast(F32), ALU.mult, ALU.subtract).then_inc(s["att_low"], 1)

        def attention2_out(act, hp):
            act.wait_ge(s["o2_ps"], 4 * (hp + 1))
            act.activation(at_hi[:, hp, :], ps[:, 6 + hp % 2, 0:TOK], ACT.Copy).then_inc(s["o2_sb"], 1)

        def attention2_low(dve, hp):
            dve.wait_ge(s["o2_sb"], hp + 1)
            dve.tensor_tensor(at_lo[:, hp, :], ps[:, 6 + hp % 2, 0:TOK], at_hi[:, hp, :].bitcast(F32), ALU.subtract
                              ).then_inc(s["o2_low"], 1)

        def gate_out(act, m):
            act.wait_ge(s["g_ps"], m + 1)
            act.activation(gate[:, m, :], ps[:, m % 2, :], ACT.Copy).then_inc(s["g_sb"], 1)

        def ffn_splits(m):
            at = ffn_slot(m)
            after = B2 + FFN_SLOTS if m == F2T - 1 else ffn_slot(m + 1)
            return [n for n in range(at + 2, after + 2) if n < B2 + FFN_SLOTS]

        def ffn_slot(m):
            return B2 + m if m < 2 else B2 + 2 + 3 * ((m - 2) // 2) + m % 2

        TILES = [(0, META, 0), (1, P, META), (2, P, META + P)]

        block = ctx.enter_context(nc.Block())

        @block.sync
        def _(sp):
            sp.dma_start(h[:, 0, :], x[0:P, :]).then_inc(x_in, 16)
            sp.dma_start(h[:, 1, :], x[P:TOK, :]).then_inc(x1_in, 16)
            sp.dma_start(cst[:, 0:C_FIRST], consts[:, 0:C_FIRST]).then_inc(const_in, 16)
            sp.dma_start(vec[:], small).then_inc(const_in, 16)
            for n in range(B1):
                if 0 <= n - SLOTS < Q_SLOT:
                    sp.wait_ge(s["wlo_done"], 2 * (n - SLOTS + 1))
                elif n >= SLOTS:
                    sp.wait_ge(used, n - SLOTS + 1)
                sp.dma_start(ring[:, n % SLOTS, :], stream[n]).then_inc(full[n % SLOTS], 16)
            for k in range(MOE_GROUP):
                n = B1 + k
                split = n - SLOTS - 2
                if Q_SLOT <= split < SPLIT1:
                    sp.wait_ge(s["wlo_done"], 2 * (split + 1))
                else:
                    sp.wait_ge(used, n - SLOTS + 1)
                sp.dma_start(ring[:, n % SLOTS, :], stream[n]).then_inc(full[n % SLOTS], 16)
            sp.wait_ge(s["rounds_done"], 1)
            rounds = sp.value_load(rounds_i[0:1, 0:1], min_val=1, max_val=GROUPS)
            with sp.Fori(1, rounds * GROUPS) as it:
                g = sp.snap(it % GROUPS)
                for k in range(MOE_GROUP):
                    n = B1 + k
                    sp.wait_ge(used, it * MOE_GROUP + (n - SLOTS + 1))
                    sp.dma_start(ring[:, n % SLOTS, :],
                                 stream[bass.ds(g * MOE_GROUP + n, 1)].rearrange("a p f -> p (a f)")
                                 ).then_inc(full[n % SLOTS], 16)
            for n in range(B2 + FFN_SLOTS):
                if n < SLOTS:
                    sp.wait_ge(used, rounds * (GROUPS * MOE_GROUP) + (B1 + n - SLOTS + 1))
                else:
                    sp.wait_ge(s["wlo_done"], 2 * (SPLIT1 + n - SLOTS + 1))
                sp.dma_start(ring[:, place2(n), :], stream[B1 + GROUPS * MOE_GROUP + n]
                             ).then_inc(full2[n % SLOTS], 16)
            for i in range(NT):
                for n in range(2):
                    sp.wait_ge(s["y_done"], 2 * i + n + 1)
                    sp.dma_start(out[i * P:(i + 1) * P, n * 512:(n + 1) * 512], xn2[:, i, n * 512:(n + 1) * 512]
                                 ).then_inc(out_st, 16)
            sp.wait_ge(out_st, 16 * 2 * NT)

        @block.scalar
        def _(act):
            act.dma_start(meta_raw, meta).then_inc(x_in, 16)
            act.dma_start(pos_i[:], positions).then_inc(const_in, 16)

            act.wait_ge(x_in, 32)
            act.wait_ge(s["init"], 1)
            act.activation(xn[0:META, 0, :], meta_raw, ACT.Square, accum_out=ssx[0:META, 0:1])
            act.activation(xn[:, 1, :], h[:, 0, :], ACT.Square, accum_out=ssx[:, 1:2])
            act.wait_ge(x1_in, 16)
            act.activation(xn[:, 2, :], h[:, 1, :], ACT.Square, accum_out=ssx[:, 2:3]).then_inc(s["ss_done"], 1)

            act.wait_ge(s["sin_in"], 1)
            act.activation(tabs[:, 1, :], tabs[:, 4, :], ACT.Sin)
            act.activation(tabs[:, 0, :], tabs[:, 5, :], ACT.Sin).then_inc(s["tab_done"], 1)
            act.dma_start(cst[:, C_FIRST:], consts[:, C_FIRST:]).then_inc(const2_in, 16)
            act.dma_start(gain[:], gains[:, 0, :]).then_inc(gain_in, 16)

            split_high(act, 0)
            for t in range(DT):
                act.wait_ge(s["turn_ps"], t + 1)
                act.activation(x_hi[:, t, :], ps[:, t, 0:COLS], ACT.Copy,
                               scale=vec[:, V_GMIX + t:V_GMIX + t + 1]).then_inc(s["turn_act"], 1)
            split_high(act, 1)
            split_high(act, 2)

            for i, m, _ in TILES:
                act.wait_ge(s["z_ps"], i + 1)
                act.activation(xn[0:m, i, 0:KVL], ps[0:m, i, QL:QL + KVL], ACT.Square, accum_out=ssz[0:m, i:i + 1])
                if i:
                    act.activation(xn[0:m, i, KVL:KVL + QL], ps[0:m, i, 0:QL], ACT.Square,
                                   accum_out=ssz[0:m, 2 + i:3 + i])
                q0 = 0 if i else QL
                act.activation(zt[0:m, i, q0:ZA], ps[0:m, i, q0:ZA], ACT.Copy).then_inc(s["z_sb"], 1)
            split_high(act, 3)

            for m in range(CT):
                act.wait_ge(s["conv_ps"], 3 * m + 1)
                if m >= 2:
                    act.wait_ge(s["conv_done"], m - 1)
                act.activation(gct[:, m % 2, :], ps[:, conv_bank(m, 0), 0:COLS], ACT.Copy).then_inc(s["gc_sb"], 1)
                for k in early_splits[m]:
                    split_high(act, k)
                if m:
                    act.wait_ge(s["conv_done"], m)
                    act.activation(sq[:, CT + m - 1, :], mrg[:, m - 1, :], ACT.Square).then_inc(s["sq_done"], 1)
                for k in late_splits[m]:
                    split_high(act, k)
            act.wait_ge(s["conv_done"], CT)
            act.activation(sq[:, 2 * CT - 1, :], mrg[:, CT - 1, :], ACT.Square).then_inc(s["sq_done"], 1)

            act.wait_ge(s["t3_ps"], 1)
            for f in range(QL // P):
                act.activation(cqT[:, f, :], ps[:, 1, f * TOK:(f + 1) * TOK], ACT.Copy,
                               scale=vec[:, V_GQ + f:V_GQ + f + 1]).then_inc(s["c_sb"], 1)
            act.wait_ge(s["t3_ps"], 2)
            act.activation(ckvT, ps[:, 2, 0:COLS], ACT.Copy, scale=vec[:, V_GKV:V_GKV + 1]).then_inc(s["c_sb"], 1)

            act.wait_ge(s["t3_ps"], 3)
            act.activation(kT[NOPE:QKD, :, :], ps[NOPE:QKD, 3, 0:COLS].unsqueeze(1).to_broadcast([ROPE, HEADS, COLS]),
                           ACT.Copy).then_inc(s["kr_sb"], 1)
            split_high_half(act, 8, 0)
            for i in range(NT):
                act.wait_ge(s["q_ps"], i + 1)
                act.activation(qtok[:, i, :], two_banks(4 + 2 * i)[:, 0:HEADS * QKD], ACT.Copy).then_inc(s["q_sb"], 1)
            split_high_half(act, 8, 1)
            for i, m in enumerate((P, P, META)):
                act.wait_ge(s["v_ps"], i + 1)
                act.activation(v1[0:m, i, :], ps[0:m, 4 + i, :], ACT.Copy).then_inc(s["v_sb"], 1)
            for hp in range(0, HEADS // 2, 2):
                act.wait_ge(s["qt_ps"], hp + 1)
                act.activation(qT[0:QKD, 2 * hp:2 * hp + 2, :], ps[0:QKD, hp, :].rearrange("p (a b) -> p a b", b=TOK),
                               ACT.Copy).then_inc(s["qt_act"], 1)

            split_high_half(act, 9, 0)
            for u in range(2 * HEADS + 1):
                if u < 2 * HEADS:
                    nk = META + P if u % 2 == 0 else COLS
                    act.wait_ge(s["nm_done"], u + 1)
                    act.activation(pm1[:, u % 3, 0:nk], pm1[:, u % 3, 0:nk], ACT.Exp, bias=nmx[:, u:u + 1],
                                   accum_out=psum_[:, u:u + 1]).then_inc(s["e_done"], 1)
                if u == 0:
                    split_high_half(act, 9, 1)
                if u:
                    w = u - 1
                    act.wait_ge(s["pt_ps"], w + 1)
                    full_k = P if w % 2 == 0 else 2 * P
                    act.activation(pt1[:, w % 2, 0:full_k], ps[:, 3 + w % 2, 0:full_k], ACT.Copy)
                    act.activation(pt1[0:META, w % 2, full_k:full_k + P], ps[0:META, 3 + w % 2, full_k:full_k + P],
                                   ACT.Copy).then_inc(s["pt_sb"], 1)
                    if w >= 4 and w % 4 == 0:
                        attention_out(act, w // 4 - 1)
                    if FILL <= w < FILL + 4 * NT and (w - FILL) % 2:
                        j = (w - FILL) // 2
                        act.wait_ge(s["cm_ps"], j + 1)
                        act.activation(cmix[:, j, :], ps[:, 5, :], ACT.Copy).then_inc(s["cm_sb"], 1)
                    if w in (FILL + 4 * NT, FILL + 4 * NT + 1):
                        split_high_half(act, 10, w - FILL - 4 * NT)
                    if w in (FILL + 4 * NT + 2, FILL + 4 * NT + 3):
                        split_high_half(act, 11, w - FILL - 4 * NT - 2)
            attention_out(act, CT - 1)

            for i in range(NT):
                act.wait_ge(s["mix_done"], 2 * i + 2)
                act.activation(xn1[:, i, :], mix[:, i, :], ACT.Square, accum_out=ssa[:, i:i + 1]).then_inc(s["ss_done"], 1)
            for i in range(NT):
                act.wait_ge(s["h1_done"], i + 1)
                act.activation(xn1[:, i, :], h[:, i, :], ACT.Square, accum_out=ssb[:, i:i + 1]).then_inc(s["ss_done"], 1)
            act.dma_start(gain[:], gains[:, 1, :]).then_inc(gain_in, 16)
            for i in range(NT):
                act.wait_ge(s["xn_done"], 1 + i + 1)
                act.activation(xh[:, i, :], xn1[:, i, :], ACT.Copy).then_inc(s["xh_done"], 1)
            for t in range(0, DT, 2):
                act.wait_ge(s["turn_ps"], 8 + t + 1)
                act.activation(tT[:, t, :], ps[:, t, 0:TOK], ACT.Copy,
                               scale=vec[:, V_GFFN + t:V_GFFN + t + 1]).then_inc(s["turn_act"], 1)

            act.wait_ge(s["lt_ps"], 1)
            act.activation(logT[0:GROUPS + EXPERTS, :], ps[0:GROUPS + EXPERTS, 7, 0:TOK], ACT.Copy).then_inc(s["lt_sb"], 1)
            act.wait_ge(s["route_a"], 1)
            act.activation(route[:, 1, 0:NT * GROUPS], route[:, 1, 0:NT * GROUPS], ACT.Exp).then_inc(s["route_b"], 1)
            act.wait_ge(s["route_c"], 1)
            act.activation(route[:, 12, 0:NT], route[:, 12, 0:NT], ACT.Exp).then_inc(s["route_d"], 1)

            for f in range(2):
                act.wait_ge(s["sgu_ps"], f + 1)
                act.activation(sg_s[:, f, :], ps[:, 4 + f, 0:TOK], ACT.Silu).then_inc(s["ssg_done"], 1)

            act.wait_ge(s["rounds_done"], 1)
            rounds = act.value_load(rounds_i[0:1, 0:1], min_val=1, max_val=GROUPS)
            with act.Fori(0, rounds) as r:
                with act.Fori(0, GROUPS) as g:
                    it = act.snap(r * GROUPS + g)
                    for t in range(0, DT, 2):
                        act.wait_ge(s["xg_ps"], it * DT + (t + 1))
                        act.activation(xg[:, t, :], ps[:, gather_bank(t), :], ACT.Copy,
                                       scale=vec[:, V_GFFN + t:V_GFFN + t + 1]).then_inc(s["xg_act"], 1)
                    for p in range(PAIRS + 1):
                        if p < PAIRS:
                            act.wait_ge(s["gu_ps"], it * PAIRS + (p + 1))
                            act.activation(sg, ps[:, 4 + p % 2, 0:FF], ACT.Silu).then_inc(s["sg_done"], 1)
                        if p:
                            for n in range(2):
                                act.wait_ge(s["y_ps"], it * (2 * PAIRS) + (2 * (p - 1) + n + 1))
                                act.activation(yh[:, n * 512:(n + 1) * 512], ps[:, 6 + n, :], ACT.Copy,
                                               scale=wsl[:, p - 1:p]).then_inc(s["yh_done"], 1)
                        if p < PAIRS:
                            act.wait_ge(s["ht_ps"], it * PAIRS + (p + 1))
                            act.activation(hid, ps[:, 4 + p % 2, 0:FF].rearrange("p (a b) -> p a b", b=P), ACT.Copy
                                           ).then_inc(s["hid_done"], 1)

            act.wait_ge(s["moe_done"], rounds * GROUPS)
            for i in range(NT):
                act.activation(squares[i], two_banks(2 * i), ACT.Square, accum_out=ssc[:, i:i + 1]).then_inc(s["ss_done"], 1)
            split_high(act, SPLIT1)
            for i in range(NT):
                act.wait_ge(s["h2_done"], i + 1)
                act.activation(xn2[:, i, :], h[:, i, :], ACT.Square, accum_out=ssd[:, i:i + 1]).then_inc(s["ss_done"], 1)
            act.dma_start(gain[:], gains[:, 2, :]).then_inc(gain_in, 16)
            for t in range(DT):
                act.wait_ge(s["turn_ps"], 16 + t + 1)
                act.activation(u_hi[:, t, :], ps[:, t, 0:TOK], ACT.Copy,
                               scale=vec[:, V_GMIX2 + t:V_GMIX2 + t + 1]).then_inc(s["turn_act"], 1)
            split_high(act, SPLIT1 + 1)

            act.wait_ge(s["zpad_done"], 1)
            for c in range(4):
                act.wait_ge(s["z2_ps"], c + 1)
                act.activation(zp[:, c, PAD:PAD + TOK], ps[:, c, 0:TOK], ACT.Copy).then_inc(s["z2_sb"], 1)
                if c % 2:
                    split_high(act, SPLIT1 + 2 + c // 2)
            for c in range(CT):
                act.wait_ge(s["q2_ps"], c + 1)
                act.activation(q2T[:, c, :], ps[:, 4 + c, 0:TOK], ACT.Copy, scale=HD ** -0.5).then_inc(s["q2_sb"], 1)
                if c % 2:
                    split_high(act, SPLIT1 + 4 + c // 2)
            for c in range(2):
                act.wait_ge(s["k2_ps"], c + 1)
                act.activation(k2T[:, c, :], ps[:, c, 0:TOK], ACT.Copy).then_inc(s["k2_sb"], 1)
            split_high(act, SPLIT1 + 6)
            act.wait_ge(s["v2_ps"], 1)
            act.activation(v2, ps[:, 2, 0:2 * P].rearrange("p (a b) -> p a b", b=P), ACT.Copy).then_inc(s["v2_sb"], 1)

            for u in range(2 * HEADS + 1):
                if u < 2 * HEADS:
                    hd = u // 2
                    act.wait_ge(s["nm2_done"], u + 1)
                    act.activation(pm2[:, u % 3, :], pm2[:, u % 3, :], ACT.Exp, bias=nmx[:, u:u + 1],
                                   accum_out=psum_[:, u:u + 1])
                    act.activation(esink[:, u:u + 1], vec[:, V_SINK + hd:V_SINK + hd + 1], ACT.Exp,
                                   bias=nmx[:, u:u + 1]).then_inc(s["e2_done"], 1)
                if u:
                    w = u - 1
                    act.wait_ge(s["pt2_ps"], w + 1)
                    act.activation(pt2[:, w % 2, :], ps[:, 4 + w % 2, 0:TOK], ACT.Copy).then_inc(s["pt2_sb"], 1)
                    if w >= 4 and w % 4 == 0:
                        attention2_out(act, w // 4 - 1)
                    if w % 2 == 1:
                        gate_out(act, w // 2)
                if u < 2 * HEADS:
                    split_high_half(act, SPLIT1 + 7 + u // 2, u % 2)
            attention2_out(act, CT - 1)
            for m in range(4):
                act.wait_ge(s["yp_ps"], m + 1)
                act.activation(yp_hi[:, m, :], ps[:, (4, 5, 0, 1)[m], 0:TOK], ACT.Copy,
                               scale=vec[:, V_PSC + m:V_PSC + m + 1]).then_inc(s["yp_sb"], 1)
            for m in range(DT):
                act.wait_ge(s["g_sb"], m + 1)
                act.activation(gate[:, m, :], gate[:, m, :], ACT.Sigmoid).then_inc(s["sig_done"], 1)
            for m in range(DT):
                if m % 2 == 0:
                    split_high(act, SPLIT1 + 15 + m // 2)
                act.wait_ge(s["mg_sum"], m + 1)
                act.activation(mg_hi[:, m, :], gate[:, m, 0:TOK], ACT.Copy).then_inc(s["mg_high"], 1)
            for n in range(19, B2 + 1):
                split_high(act, SPLIT1 + n)
            for i in range(NT):
                act.wait_ge(s["h3_done"], i + 1)
                act.activation(xn2[:, i, :], h[:, i, :], ACT.Square, accum_out=sse[:, i:i + 1]).then_inc(s["ss_done"], 1)
            for t in range(DT):
                act.wait_ge(s["turn_ps"], 24 + t + 1)
                act.activation(u_hi[:, t, :], ps[:, t, 0:TOK], ACT.Copy,
                               scale=vec[:, V_GFFN2 + t:V_GFFN2 + t + 1]).then_inc(s["turn_act"], 1)
            split_high(act, SPLIT1 + B2 + 1)

            for m in range(F2T):
                act.wait_ge(s["f_ps"], m + 1)
                act.activation(fsg[:, m % 4, :], ps[:, 4 + m % 4, 0:TOK], ACT.Silu).then_inc(s["fsg_done"], 1)
                act.wait_ge(s["fh_sum"], m + 1)
                act.activation(fh_hi[:, m % 4, :], fh[:, m % 4, :], ACT.Copy).then_inc(s["fh_high"], 1)
                for n in ffn_splits(m):
                    split_high(act, SPLIT1 + n)
            for i in range(NT):
                act.wait_ge(s["h4_done"], i + 1)
                act.activation(xn2[:, i, :], h[:, i, :], ACT.Square, accum_out=ssf[:, i:i + 1]).then_inc(s["ss_done"], 1)

        @block.gpsimd
        def _(pool):
            steps = [0]

            def rstd(ss, ms, rs, n, done):
                pool.tensor_scalar(ms, ss, 1.0 / n, EPS, ALU.mult, ALU.add).then_inc(s["pool_step"], 1)
                steps[0] += 1
                pool.wait_ge(s["pool_step"], steps[0])
                power(ms, rs).then_inc(done, 1)

            def power(ms, rs):
                return pool.tensor_tensor(rs, ms, cst[:, C_NHALF:C_NHALF + 1].to_broadcast([P, rs.shape[1]]), ALU.pow)

            pool.wait_ge(const_in, 48)
            pool.wait_ge(s["ss_done"], 1)
            rstd(ssx, msx, rsx, D, s["rs_done"])
            pool.wait_ge(s["z_sb"], 3)
            pool.tensor_scalar(msz[:, 0:3], ssz[:, 0:3], 1.0 / KVL, EPS, ALU.mult, ALU.add).then_inc(s["pool_step"], 1)
            pool.tensor_scalar(msz[:, 3:5], ssz[:, 3:5], 1.0 / QL, EPS, ALU.mult, ALU.add).then_inc(s["pool_step"], 1)
            steps[0] += 2
            pool.wait_ge(s["pool_step"], steps[0])
            power(msz, rsz).then_inc(s["rz_done"], 1)
            for m in range(CT):
                pool.wait_ge(s["sq_done"], m + 1)
                pool.tensor_scalar(mrg[:, m, :], mrg[:, m, :], vec[:, V_GCONV + m:V_GCONV + m + 1], 1.0,
                                   ALU.mult, ALU.mult).then_inc(s["pool_step"], 1)
                steps[0] += 1
            pool.wait_ge(s["pool_step"], steps[0])
            pool.wait_ge(s["conv_ps"], 3 * CT)
            for m in range(CT):
                pool.tensor_copy(mrg_hi[:, CT + m, :], mrg[:, m, :]).then_inc(s["pool_step"], 1)
                steps[0] += 1
                pool.wait_ge(s["pool_step"], steps[0])
                pool.tensor_tensor(mrg_lo[:, CT + m, :], mrg[:, m, :], mrg_hi[:, CT + m, :].bitcast(F32), ALU.subtract
                                   ).then_inc(s["convg_done"], 1)

            def add_squares(to, other):
                pool.tensor_tensor(sq[:, to, :], sq[:, to, :], sq[:, other, :], ALU.add).then_inc(s["sqs_done"], 1)

            split_low(pool, 8)
            for k in range(1, CT):
                if k > 1:
                    pool.wait_ge(s["sqs_done"], k - 1)
                add_squares(CT, CT + k)
            split_low(pool, 9)
            for k in range(1, CT - 1):
                pool.wait_ge(s["sq_done"], CT + k + 1)
                if k > 1:
                    pool.wait_ge(s["sqs_done"], CT - 1 + k - 1)
                    split_low(pool, 10)
                add_squares(0, k)
            split_low(pool, 11)
            pool.wait_ge(s["msm_done"], 1)
            power(msm, rsm).then_inc(s["rsm_done"], 1)
            for k, (ss, ms, rs) in enumerate(((ssa, msa, rsa), (ssb, msb, rsb), (ssc, msc, rsc), (ssd, msd, rsd))):
                for i in range(NT):
                    pool.wait_ge(s["ss_done"], 1 + NT * k + i + 1)
                    rstd(ss[:, i:i + 1], ms[:, i:i + 1], rs[:, i:i + 1], D, s["rs_done"])

            pool.wait_ge(const2_in, 16)
            for c, w in enumerate(POOL_WINDOWS):
                pool.wait_ge(s["z2_sb"], c + 1)
                src, half, k, wide = zp[:, c, :], 1, 0, TOK + 2 * PAD
                while half < w:
                    back, ahead = (1, 0) if half == 1 else (half // 2, half // 2)
                    lo, hi = half, wide - half + 1
                    pool.tensor_tensor(win[:, k % 2, lo:hi], src[:, lo - back:hi - back],
                                       src[:, lo + ahead:hi + ahead], ALU.add).then_inc(s["pool_step"], 1)
                    steps[0] += 1
                    pool.wait_ge(s["pool_step"], steps[0])
                    src, half, k = win[:, k % 2, :], 2 * half, k + 1
                pool.tensor_tensor(dp[:, c, :], src[:, PAD:PAD + TOK], cst[:, C_CNT + c * TOK:C_CNT + (c + 1) * TOK],
                                   ALU.mult).then_inc(s["pool_step"], 1)
                steps[0] += 1
                pool.wait_ge(s["pool_step"], steps[0])
                pool.tensor_tensor(dp[:, c, :], dp[:, c, :], zp[:, c, PAD:PAD + TOK], ALU.subtract).then_inc(s["dp_done"], 1)
            for k, (ss, ms, rs) in enumerate(((sse, mse, rse), (ssf, msf, rsf))):
                for i in range(NT):
                    pool.wait_ge(s["ss_done"], 1 + NT * (4 + k) + i + 1)
                    rstd(ss[:, i:i + 1], ms[:, i:i + 1], rs[:, i:i + 1], D, s["rs_done"])

        @block.vector
        def _(dve):
            steps = [0]

            def link(ins):
                ins.then_inc(s["dve_step"], 1)
                steps[0] += 1
                dve.wait_ge(s["dve_step"], steps[0])

            def halves(a, w):
                return a.rearrange("p (a b) -> p a b", b=w)

            dve.memset(stat[:], 1.0)
            dve.memset(zt[:, 0, :], 0.0)
            dve.memset(kr, 0.0).then_inc(s["init"], 1)

            dve.wait_ge(const_in, 48)
            dve.wait_ge(s["init"], 1)
            dve.tensor_copy(posf[:, 0:1], cst[:, C_POS:C_POS + 1])
            link(dve.tensor_copy(posf[:, 1:3], pos_i[:]))
            link(dve.tensor_scalar(posf[:, 1:3], posf[:, 1:3], float(META), None, ALU.add))
            NR = ROPE // 2
            ang, kk, red, co, ab = (tabs[:, j, :] for j in (2, 3, 4, 5, 6))
            link(dve.tensor_tensor(halves(ang, NR), cst[:, C_FREQ:C_FREQ + NR].unsqueeze(1).to_broadcast([P, 3, NR]),
                                   posf.unsqueeze(2).to_broadcast([P, 3, NR]), ALU.mult))
            link(dve.tensor_scalar(kk, ang, 1.0 / TWO_PI, ROUND_MAGIC, ALU.mult, ALU.add))
            link(dve.tensor_scalar(kk, kk, -ROUND_MAGIC, None, ALU.add))
            link(dve.scalar_tensor_tensor(red, kk, -PI_1, ang, ALU.mult, ALU.add))
            link(dve.scalar_tensor_tensor(red, kk, -PI_2, red, ALU.mult, ALU.add))
            link(dve.scalar_tensor_tensor(red, kk, -PI_3, red, ALU.mult, ALU.add))
            link(dve.tensor_scalar(red, red, PI_F32, -PI_F32, ALU.min, ALU.max))
            link(dve.scalar_tensor_tensor(ab, red, -1.0, red, ALU.mult, ALU.min))
            dve.tensor_scalar(co, ab, TWO_PI / 4, None, ALU.add).then_inc(s["sin_in"], 1)

            dve.wait_ge(s["rs_done"], 1)
            dve.tensor_scalar(xn[0:META, 0, :], meta_raw, rsx[0:META, 0:1], None, ALU.mult)
            for i in range(NT):
                last = dve.tensor_scalar(xn[:, 1 + i, :], h[:, i, :], rsx[:, 1 + i:2 + i], None, ALU.mult)
            last.then_inc(s["xn_done"], 1)
            split_low(dve, 0)
            for t in range(DT):
                dve.wait_ge(s["turn_act"], t + 1)
                dve.scalar_tensor_tensor(x_lo[:, t, :], ps[:, t, 0:COLS], vec[:, V_GMIX + t:V_GMIX + t + 1],
                                         x_hi[:, t, :].bitcast(F32), ALU.mult, ALU.subtract).then_inc(s["turn_dve"], 1)
            for k in (1, 2):
                split_low(dve, k)

            def rope(x1, x2, cos, sin, o1, o2, temps):
                a, b, c, d = temps
                dve.tensor_tensor(a, x1, cos, ALU.mult)
                dve.tensor_tensor(b, x2, sin, ALU.mult)
                dve.tensor_tensor(c, x2, cos, ALU.mult)
                link(dve.tensor_tensor(d, x1, sin, ALU.mult))
                dve.tensor_tensor(o1, a, b, ALU.subtract)
                return dve.tensor_tensor(o2, c, d, ALU.add)

            dve.wait_ge(s["z_sb"], 3)
            dve.wait_ge(s["tab_done"], 1)
            z0 = QL + KVL
            rope(zt[:, :, z0:z0 + NR], zt[:, :, z0 + NR:z0 + ROPE], halves(tabs[:, 0, :], NR), halves(tabs[:, 1, :], NR),
                 kr[:, :, NOPE:NOPE + NR], kr[:, :, NOPE + NR:QKD],
                 [halves(rt[:, j, 0:3 * NR], NR) for j in range(4)]).then_inc(s["kr_done"], 1)
            dve.wait_ge(s["rz_done"], 1)
            for i in range(NT + 1):
                last = dve.tensor_scalar(zt[:, i, QL:z0], zt[:, i, QL:z0], rsz[:, i:i + 1], None, ALU.mult)
                if i:
                    last = dve.tensor_scalar(zt[:, i, 0:QL], zt[:, i, 0:QL], rsz[:, 2 + i:3 + i], None, ALU.mult)
            last.then_inc(s["zn_done"], 1)
            split_low(dve, 3)

            for m in range(CT):
                dve.wait_ge(s["gc_sb"], m + 1)
                dve.wait_ge(s["conv_ps"], 3 * m + 2)
                link(dve.tensor_tensor(u_t, gct[:, m % 2, :], ps[:, conv_bank(m, 1), 0:COLS], ALU.mult))
                w = [vec[:, V_CONV + k * CT + m:V_CONV + k * CT + m + 1] for k in range(3)]
                link(dve.tensor_scalar(cy, u_t[:, META - 2:META - 2 + TOK], w[0], None, ALU.mult))
                link(dve.scalar_tensor_tensor(cy, u_t[:, META - 1:META - 1 + TOK], w[1], cy, ALU.mult, ALU.add))
                link(dve.scalar_tensor_tensor(cy, u_t[:, META:META + TOK], w[2], cy, ALU.mult, ALU.add))
                for k in early_splits[m]:
                    split_low(dve, k)
                dve.wait_ge(s["conv_ps"], 3 * m + 3)
                dve.tensor_tensor(mrg[:, m, :], cy, ps[:, conv_bank(m, 2), 0:TOK], ALU.mult
                                  ).then_inc(s["conv_done"], 1)
                for k in late_splits[m]:
                    split_low(dve, k)

            def k_out(hp):
                dve.wait_ge(s["kn_ps"], hp + 1)
                for j in range(2):
                    last = dve.tensor_copy(kT[0:NOPE, 2 * hp + j, :], ps[j * NOPE:(j + 1) * NOPE, hp % 3, 0:COLS])
                last.then_inc(s["kn_sb"], 1)

            def q_rope(i):
                dve.wait_ge(s["q_sb"], i + 1)
                q = halves(qtok[:, i, :], QKD)
                c, sn = (tabs[:, j, (1 + i) * NR:(2 + i) * NR].unsqueeze(1).to_broadcast([P, HEADS, NR]) for j in (0, 1))
                x1, x2 = q[:, :, NOPE:NOPE + NR], q[:, :, NOPE + NR:QKD]
                rope(x1, x2, c, sn, x1, x2, [halves(rt[:, j, :], NR) for j in range(4)]).then_inc(s["qr_done"], 1)

            k_out(0)
            k_out(1)
            q_rope(0)
            k_out(2)
            k_out(3)
            dve.wait_ge(s["qr_done"], 1)
            q_rope(1)
            for hp in range(1, HEADS // 2, 2):
                dve.wait_ge(s["qt_ps"], hp + 1)
                dve.tensor_copy(qT[0:QKD, 2 * hp:2 * hp + 2, :], halves(ps[0:QKD, hp, :], TOK)).then_inc(s["qt_dve"], 1)

            dve.wait_ge(const2_in, 16)
            for u in range(2 * HEADS + 1):
                if u < 2 * HEADS:
                    nk = META + P if u % 2 == 0 else COLS
                    dve.wait_ge(s["s_ps"], u + 1)
                    dve.scalar_tensor_tensor(pm1[:, u % 3, 0:nk], ps[:, u % 3, 0:nk], ATTN_SCALE, mask[:, COLS - nk:COLS],
                                             ALU.mult, ALU.add).then_inc(s["s_sb"], 1)
                    dve.wait_ge(s["s_sb"], u + 1)
                    dve.tensor_reduce(nmx[:, u:u + 1], pm1[:, u % 3, 0:nk], AX.X, ALU.max, negate=True
                                      ).then_inc(s["nm_done"], 1)
                if u:
                    w = u - 1
                    nk = META + P if w % 2 == 0 else COLS
                    dve.wait_ge(s["e_done"], w + 1)
                    link(dve.reciprocal(rinv[:, w:w + 1], psum_[:, w:w + 1]))
                    dve.tensor_scalar(pm1[:, w % 3, 0:nk], pm1[:, w % 3, 0:nk], rinv[:, w:w + 1], None, ALU.mult
                                      ).then_inc(s["p_done"], 1)
                    if w >= 5 and w % 4 == 1:
                        attention_low(dve, w // 4 - 1)
            attention_low(dve, CT - 1)

            dve.wait_ge(s["ssm_ps"], 1)
            dve.tensor_scalar(msm, ps[:, 5, 0:4], 1.0 / 512, EPS, ALU.mult, ALU.add).then_inc(s["msm_done"], 1)
            dve.wait_ge(s["rsm_done"], 1)
            for j in range(2 * NT):
                dve.tensor_scalar(cmix[:, j, :], cmix[:, j, :], rsm[:, 2 * (j // 2) + 1:2 * (j // 2) + 2], None, ALU.mult
                                  ).then_inc(s["cms_done"], 1)
            for i in range(NT):
                for n in range(2):
                    j = 2 * i + n
                    dve.wait_ge(s["mix_ps"], j + 1)
                    dve.wait_ge(s["cms_done"], j + 1)
                    dve.scalar_tensor_tensor(mix[:, i, n * 512:(n + 1) * 512], ps[:, j, :], rsm[:, 2 * i:2 * i + 1],
                                             cmix[:, j, :], ALU.mult, ALU.add).then_inc(s["mix_done"], 1)
            dve.wait_ge(gain_in, 16)
            for i in range(NT):
                dve.wait_ge(s["mix_done"], 2 * i + 2)
                dve.tensor_tensor(gmix[:, i, :], mix[:, i, :], gain[:], ALU.mult).then_inc(s["gmix_done"], 1)

            for i in range(NT):
                dve.wait_ge(s["rs_done"], 1 + i + 1)
                dve.wait_ge(s["gmix_done"], i + 1)
                dve.scalar_tensor_tensor(h[:, i, :], gmix[:, i, :], rsa[:, i:i + 1], h[:, i, :], ALU.mult, ALU.add
                                         ).then_inc(s["h1_done"], 1)
            for i in range(NT):
                dve.wait_ge(s["rs_done"], 3 + i + 1)
                dve.tensor_scalar(xn1[:, i, :], h[:, i, :], rsb[:, i:i + 1], None, ALU.mult).then_inc(s["xn_done"], 1)
            for t in range(1, DT, 2):
                dve.wait_ge(s["turn_ps"], 8 + t + 1)
                dve.tensor_scalar(tT[:, t, :], ps[:, t, 0:TOK], vec[:, V_GFFN + t:V_GFFN + t + 1], None,
                                  ALU.mult).then_inc(s["turn_dve"], 1)

            def rt_(k, w):
                a = route[:, k, 0:NT * w]
                return a if w == 1 else halves(a, w)

            def wide(a, w):
                return a.unsqueeze(2).to_broadcast([P, NT, w])

            def first_max(x, k, w):
                desc = cst[:, C_DESC:C_DESC + w].unsqueeze(1).to_broadcast([P, NT, w])
                link(dve.tensor_reduce(rt_(k, 1), x, AX.X, ALU.max))
                link(dve.tensor_tensor(rt_(k + 1, w), x, wide(rt_(k, 1), w), ALU.is_equal))
                link(dve.tensor_tensor(rt_(k + 2, w), rt_(k + 1, w), desc, ALU.mult))
                link(dve.tensor_reduce(rt_(k + 3, 1), rt_(k + 2, w), AX.X, ALU.max))
                link(dve.tensor_tensor(rt_(k + 4, w), rt_(k + 2, w), wide(rt_(k + 3, 1), w), ALU.is_equal))
                return rt_(k, 1), rt_(k + 4, w)

            dve.wait_ge(s["lg_ps"], 1)
            W = GROUPS + EXPERTS
            link(dve.tensor_tensor(logit, halves(ps[:, 6, 0:NT * W], W),
                                   vec[:, V_RB:V_RB + W].unsqueeze(1).to_broadcast([P, NT, W]), ALU.add))
            gl, el = logit[:, :, 0:GROUPS], logit[:, :, GROUPS:W]
            gmax, group = first_max(gl, 2, GROUPS)
            dve.tensor_tensor(rt_(1, GROUPS), gl, wide(gmax, GROUPS), ALU.subtract).then_inc(s["route_a"], 1)
            link(dve.tensor_scalar(rt_(7, GROUPS), group, BIG, -BIG, ALU.mult, ALU.add))
            em = rt_(8, EXPERTS)
            link(dve.tensor_tensor(em.rearrange("p a (b c) -> p a b c", c=PER_GROUP),
                                   el.rearrange("p a (b c) -> p a b c", c=PER_GROUP),
                                   rt_(7, GROUPS).unsqueeze(3).to_broadcast([P, NT, GROUPS, PER_GROUP]), ALU.add))
            m1, h1 = first_max(em, 13, EXPERTS)
            link(dve.scalar_tensor_tensor(rt_(9, EXPERTS), h1, -2 * BIG, em, ALU.mult, ALU.add))
            m2, h2 = first_max(rt_(9, EXPERTS), 18, EXPERTS)
            dve.tensor_tensor(rt_(12, 1), m2, m1, ALU.subtract).then_inc(s["route_c"], 1)
            dve.tensor_tensor(chosen, h1, h2, ALU.add).then_inc(s["chosen_done"], 1)
            dve.wait_ge(s["route_b"], 1)
            link(dve.tensor_reduce(rt_(0, 1), rt_(1, GROUPS), AX.X, ALU.add))
            dve.wait_ge(s["route_d"], 1)
            link(dve.tensor_scalar(rt_(10, 1), rt_(12, 1), 1.0, None, ALU.add))
            link(dve.tensor_tensor(rt_(10, 1), rt_(10, 1), rt_(0, 1), ALU.mult))
            link(dve.reciprocal(rt_(10, 1), rt_(10, 1)))
            link(dve.tensor_tensor(rt_(11, 1), rt_(10, 1), rt_(12, 1), ALU.mult))
            link(dve.tensor_tensor(comb, h1, wide(rt_(10, 1), EXPERTS), ALU.mult))
            link(dve.tensor_tensor(rt_(9, EXPERTS), h2, wide(rt_(11, 1), EXPERTS), ALU.mult))
            link(dve.tensor_tensor(comb, comb, rt_(9, EXPERTS), ALU.add))

            for i in range(NT):
                dve.wait_ge(s["xh_done"], i + 1)
                dve.tensor_tensor(xl[:, i, :], xn1[:, i, :], xh[:, i, :].bitcast(F32), ALU.subtract).then_inc(s["xl_done"], 1)

            link(dve.tensor_scalar(rankp[:, :, 0:EXPERTS], chosen, -1e4, 1e4, ALU.mult, ALU.add))
            dve.wait_ge(s["rank_ps"], 1)
            link(dve.tensor_tensor(rankp[:, :, 0:EXPERTS], rankp[:, :, 0:EXPERTS], halves(ps[:, 7, 0:NT * EXPERTS], EXPERTS),
                                   ALU.add))
            link(dve.tensor_scalar(rankp[:, :, EXPERTS:EXPERTS + PER_GROUP], rankp[:, :, 0:PER_GROUP], -float(CAP), None,
                                   ALU.add))
            link(dve.tensor_reduce(cnt[:, 0:1], ps[:, 7, NT * EXPERTS:(NT + 1) * EXPERTS], AX.X, ALU.max))
            link(dve.tensor_scalar(cnt[:, 1:2], cnt[:, 0:1], float(CAP), 1.0, ALU.is_gt, ALU.add))
            for k in range(2, TOK // CAP):
                link(dve.scalar_tensor_tensor(cnt[:, k:k + 1], cnt[:, 0:1], float(k * CAP), cnt[:, k - 1:k],
                                              ALU.is_gt, ALU.add))
            dve.tensor_copy(rounds_i[:], cnt[:, TOK // CAP - 1:TOK // CAP]).then_inc(s["rounds_done"], 1)

            def select(ranks):
                for i in range(NT):
                    last = dve.tensor_tensor(
                        halves(sel[:, i, :], CAP), ranks[:, i, :].unsqueeze(2).to_broadcast([P, PER_GROUP, CAP]),
                        cst[:, C_IOTA:C_IOTA + CAP].unsqueeze(1).to_broadcast([P, PER_GROUP, CAP]), ALU.is_equal)
                last.then_inc(s["sel_done"], 1)

            select(rankp[:, :, 0:PER_GROUP])
            for f in range(2):
                dve.wait_ge(s["ssg_done"], f + 1)
                dve.tensor_tensor(hs[:, f, :], sg_s[:, f, :], ps[:, 4 + f, TOK:2 * TOK], ALU.mult).then_inc(s["hs_done"], 1)
            dve.wait_ge(s["rounds_done"], 1)
            rounds = dve.value_load(rounds_i[0:1, 0:1], min_val=1, max_val=GROUPS)
            with dve.Fori(0, rounds) as r:
                with dve.Fori(0, GROUPS) as g:
                    it = dve.snap(r * GROUPS + g)
                    for q in range(2):
                        dve.wait_ge(s["st_ps"], it * 3 + (q + 1))
                        dve.tensor_copy(selT[:, 2 * q:2 * q + 2, :], halves(ps[:, 4 + q, :], TOK)).then_inc(s["st_sb"], 1)
                    dve.wait_ge(s["st_ps"], it * 3 + 3)
                    dve.tensor_copy(wsl[0:CAP, :], ps[0:CAP, 6, 0:2 * PAIRS:2])
                    dve.tensor_copy(wsl[CAP:P, :], ps[CAP:P, 6, 1:2 * PAIRS:2]).then_inc(s["st_sb"], 1)
                    for t in range(1, DT, 2):
                        dve.wait_ge(s["xg_ps"], it * DT + (t + 1))
                        dve.tensor_scalar(xg[:, t, :], ps[:, gather_bank(t), :], vec[:, V_GFFN + t:V_GFFN + t + 1], None,
                                          ALU.mult).then_inc(s["xg_dve"], 1)
                    ahead = rankp[:, :, bass.ds(g * PER_GROUP + PER_GROUP, PER_GROUP)]
                    select(ahead)
                    dve.wait_ge(s["sel_done"], it + 2)
                    dve.tensor_scalar(ahead, ahead, -float(CAP), None, ALU.add).then_inc(s["rank_step"], 1)
                    for p in range(PAIRS + 1):
                        if p < PAIRS:
                            dve.wait_ge(s["sg_done"], it * PAIRS + (p + 1))
                            dve.tensor_tensor(htok, sg, ps[:, 4 + p % 2, FF:2 * FF], ALU.mult).then_inc(s["ht_done"], 1)
                        if p:
                            for n in range(2):
                                dve.wait_ge(s["yh_done"], it * (2 * PAIRS) + (2 * (p - 1) + n + 1))
                                dve.scalar_tensor_tensor(yl[:, n * 512:(n + 1) * 512], ps[:, 6 + n, :], wsl[:, p - 1:p],
                                                         yh[:, n * 512:(n + 1) * 512].bitcast(F32), ALU.mult, ALU.subtract
                                                         ).then_inc(s["yl_done"], 1)
                    dve.wait_ge(s["rank_step"], it + 1)

            dve.wait_ge(gain_in, 32)
            dve.tensor_scalar(nsink, vec[:, V_SINK:V_SINK + HEADS], -1.0, None, ALU.mult)
            dve.memset(win, 0.0)
            dve.memset(zp, 0.0).then_inc(s["zpad_done"], 1)
            for i in range(NT):
                dve.wait_ge(s["ss_done"], 5 + i + 1)
                dve.tensor_tensor(mixb[:, i, :], two_banks(2 * i), gain[:], ALU.mult).then_inc(s["gmoe_done"], 1)
            for i in range(NT):
                dve.wait_ge(s["rs_done"], 5 + i + 1)
                dve.wait_ge(s["gmoe_done"], i + 1)
                dve.scalar_tensor_tensor(h[:, i, :], mixb[:, i, :], rsc[:, i:i + 1], h[:, i, :], ALU.mult, ALU.add
                                         ).then_inc(s["h2_done"], 1)
            split_low_half(dve, SPLIT1, 0)
            for i in range(NT):
                dve.wait_ge(s["rs_done"], 7 + i + 1)
                dve.tensor_scalar(xn2[:, i, :], h[:, i, :], rsd[:, i:i + 1], None, ALU.mult).then_inc(s["xn_done"], 1)
            split_low_half(dve, SPLIT1, 1)
            for t in range(DT):
                dve.wait_ge(s["turn_act"], 12 + t + 1)
                dve.scalar_tensor_tensor(u_lo[:, t, :], ps[:, t, 0:TOK], vec[:, V_GMIX2 + t:V_GMIX2 + t + 1],
                                         u_hi[:, t, :].bitcast(F32), ALU.mult, ALU.subtract).then_inc(s["turn_dve"], 1)
            for n in range(1, 7):
                split_low(dve, SPLIT1 + n)

            for u in range(2 * HEADS + 1):
                if u < 2 * HEADS:
                    hd, i = u // 2, u % 2
                    dve.wait_ge(s["s2_ps"], u + 1)
                    dve.scalar_tensor_tensor(pm2[:, u % 3, :], cst[:, C_DIST + i * TOK:C_DIST + (i + 1) * TOK],
                                             -(2.0 ** (-8.0 * (hd + 1) / HEADS)), ps[:, 2 + u % 2, 0:TOK],
                                             ALU.mult, ALU.add).then_inc(s["s2_sb"], 1)
                    dve.wait_ge(s["s2_sb"], u + 1)
                    link(dve.tensor_reduce(rinv[:, u:u + 1], pm2[:, u % 3, :], AX.X, ALU.max, negate=True))
                    dve.tensor_tensor(nmx[:, u:u + 1], rinv[:, u:u + 1], nsink[:, hd:hd + 1], ALU.min
                                      ).then_inc(s["nm2_done"], 1)
                if u:
                    w = u - 1
                    dve.wait_ge(s["e2_done"], w + 1)
                    link(dve.tensor_tensor(psum_[:, w:w + 1], psum_[:, w:w + 1], esink[:, w:w + 1], ALU.add))
                    link(dve.reciprocal(rinv[:, w:w + 1], psum_[:, w:w + 1]))
                    dve.tensor_scalar(pm2[:, w % 3, :], pm2[:, w % 3, :], rinv[:, w:w + 1], None, ALU.mult
                                      ).then_inc(s["p2_done"], 1)
                    if w >= 5 and w % 4 == 1:
                        attention2_low(dve, w // 4 - 1)
                if u:
                    split_low_half(dve, SPLIT1 + 7 + (u - 1) // 2, (u - 1) % 2)

            attention2_low(dve, CT - 1)
            for m in range(4):
                dve.wait_ge(s["yp_sb"], m + 1)
                dve.scalar_tensor_tensor(yp_lo[:, m, :], ps[:, (4, 5, 0, 1)[m], 0:TOK], vec[:, V_PSC + m:V_PSC + m + 1],
                                         yp_hi[:, m, :].bitcast(F32), ALU.mult, ALU.subtract).then_inc(s["yp_low"], 1)
            for m in range(DT):
                if m % 2 == 0:
                    split_low(dve, SPLIT1 + 15 + m // 2)
                dve.wait_ge(s["sig_done"], m + 1)
                dve.wait_ge(s["br_ps"], m + 1)
                dve.tensor_tensor(gate[:, m, :], gate[:, m, :], ps[:, 2 + m % 4, :], ALU.mult).then_inc(s["br_sb"], 1)
                dve.wait_ge(s["br_sb"], m + 1)
                dve.tensor_tensor(gate[:, m, 0:TOK], gate[:, m, 0:TOK], gate[:, m, TOK:2 * TOK], ALU.add
                                  ).then_inc(s["mg_sum"], 1)
                dve.wait_ge(s["mg_high"], m + 1)
                dve.tensor_tensor(mg_lo[:, m, :], gate[:, m, 0:TOK], mg_hi[:, m, :].bitcast(F32), ALU.subtract
                                  ).then_inc(s["mg_done"], 1)
            for n in range(19, B2 + 1):
                split_low(dve, SPLIT1 + n)
            for i in range(NT):
                dve.wait_ge(s["h3_ps"], i + 1)
                dve.tensor_tensor(h[:, i, :], h[:, i, :], two_banks(6 * i), ALU.add).then_inc(s["h3_done"], 1)
            for i in range(NT):
                dve.wait_ge(s["rs_done"], 9 + i + 1)
                dve.tensor_scalar(xn2[:, i, :], h[:, i, :], rse[:, i:i + 1], None, ALU.mult).then_inc(s["xn_done"], 1)
            for t in range(DT):
                dve.wait_ge(s["turn_act"], 20 + t + 1)
                dve.scalar_tensor_tensor(u_lo[:, t, :], ps[:, t, 0:TOK], vec[:, V_GFFN2 + t:V_GFFN2 + t + 1],
                                         u_hi[:, t, :].bitcast(F32), ALU.mult, ALU.subtract).then_inc(s["turn_dve"], 1)
            split_low(dve, SPLIT1 + B2 + 1)
            for m in range(F2T):
                dve.wait_ge(s["fsg_done"], m + 1)
                dve.tensor_tensor(fh[:, m % 4, :], fsg[:, m % 4, :], ps[:, 4 + m % 4, TOK:2 * TOK], ALU.mult
                                  ).then_inc(s["fh_sum"], 1)
                dve.wait_ge(s["fh_high"], m + 1)
                dve.tensor_tensor(fh_lo[:, m % 4, :], fh[:, m % 4, :], fh_hi[:, m % 4, :].bitcast(F32), ALU.subtract
                                  ).then_inc(s["fh_done"], 1)
                for n in ffn_splits(m):
                    split_low(dve, SPLIT1 + n)
            for i in range(NT):
                dve.wait_ge(s["facc_ps"], i + 1)
                dve.tensor_tensor(h[:, i, :], h[:, i, :], two_banks(2 * i), ALU.add).then_inc(s["h4_done"], 1)
            dve.wait_ge(gain_in, 48)
            for i in range(NT):
                dve.wait_ge(s["rs_done"], 11 + i + 1)
                for n in range(2):
                    a = slice(n * 512, (n + 1) * 512)
                    dve.scalar_tensor_tensor(xn2[:, i, a], h[:, i, a], rsf[:, i:i + 1], gain[:, a], ALU.mult, ALU.mult
                                             ).then_inc(s["y_done"], 1)

        @block.tensor
        def _(pe):
            def mm(o, lhsT, rhs, start, stop, **kw):
                return pe.matmul(o, lhsT, rhs, start=start, stop=stop, **kw)

            def turn(o, a, rows=P):
                return pe.transpose(o, a, ident[0:rows, 0:rows])

            def split_ready(k, half):
                pe.wait_ge(s["wlo_done"], 2 * k + half + 1)

            def triple(o, stat_hl, mov_hl, first, last_k):
                (ah, al), (bh, bl) = stat_hl, mov_hl
                begin = mm(o, ah, bh, first, False, skip_group_check=True)
                mm(o, ah, bl, False, False, skip_group_check=True)
                return begin, mm(o, al, bh, False, last_k, skip_group_check=True)

            def chunk(o, k, half, acts, frees=0, turned_from=None, bank=0):
                split_ready(k, half)
                for t in range(DT):
                    if turned_from is not None:
                        pe.wait_ge(s["turn_dve"], turned_from + max(t, bank) + 1)
                    c = half * D + t * P
                    begin, last = triple(o, [w[k % 2][:, c:c + P] for w in (w_hi, w_lo)], [a[:, t] for a in acts],
                                         t == 0, t == DT - 1)
                    if t == 0 and frees:
                        begin.then_inc(split_used, frees)
                return last

            pe.wait_ge(const_in, 48)
            pe.wait_ge(s["xn_done"], 1)
            for t in range(DT):
                turn(ps[:, t, 0:META], xn[0:META, 0, t * P:(t + 1) * P], META)
                turn(ps[:, t, META:META + P], xn[:, 1, t * P:(t + 1) * P])
                turn(ps[:, t, META + P:COLS], xn[:, 2, t * P:(t + 1) * P]).then_inc(s["turn_ps"], 1)

            for t in range(DT):
                split_ready(t // 4, (t % 4) * ZA // D if t % 4 < 2 else 1)
                pe.wait_ge(s["turn_dve"], max(t + 1, 3))
                for i, m, c in TILES:
                    q0 = 0 if i else QL
                    w = [a[t // 4][:, (t % 4) * ZA + q0:(t % 4 + 1) * ZA] for a in (w_hi, w_lo)]
                    begin, last = triple(ps[0:m, i, q0:ZA], [x[:, t, c:c + m] for x in (x_hi, x_lo)], w, t == 0, t == DT - 1)
                    if t == 4 and i == 0:
                        begin.then_inc(split_used, 1)
                    if t == DT - 1:
                        last.then_inc(s["z_ps"], 1)

            for c in range(3 * CT):
                m, kind = c // 3, c % 3
                if m == 1 and kind == 2:
                    pe.wait_ge(s["z_sb"], 1)
                if m >= 2 and kind == 0:
                    pe.wait_ge(s["conv_done"], m - 1)
                lo, w = (META, TOK) if kind == 2 else (0, COLS)
                chunk(ps[:, conv_bank(m, kind), 0:w], 2 + c // 2, c % 2, [x[:, :, lo:lo + w] for x in (x_hi, x_lo)],
                      frees=1 - c % 2).then_inc(s["conv_ps"], 1)

            pe.wait_ge(s["zn_done"], 1)
            pe.wait_ge(s["z_sb"], 3)
            for f in range(QL // P):
                for i in range(NT):
                    last = turn(ps[:, 1, f * TOK + i * P:f * TOK + (i + 1) * P], zt[:, 1 + i, f * P:(f + 1) * P])
                    if f == 0 and i == 0:
                        last.then_inc(split_used, 1)
            last.then_inc(s["t3_ps"], 1)
            for i, m, c in TILES:
                last = turn(ps[:, 2, c:c + m], zt[0:m, i, QL:QL + KVL], m)
            last.then_inc(s["t3_ps"], 1)
            pe.wait_ge(s["kr_done"], 1)
            pe.wait_ge(s["conv_done"], CT - 1)
            for i, m, c in TILES:
                last = turn(ps[0:QKD, 3, c:c + m], kr[0:m, i, :], m)
            last.then_inc(s["t3_ps"], 1)

            slot_ready(pe, 9)
            wkv = ring[:, 9 % SLOTS, :]
            pe.wait_ge(s["c_sb"], 3)
            pe.wait_ge(s["conv_done"], CT - 1)

            def k_pair(hp):
                if hp >= 3:
                    pe.wait_ge(s["kn_sb"], hp - 2)
                mm(ps[:, hp % 3, 0:COLS], wkv[:, hp * P:(hp + 1) * P], ckvT, True, True).then_inc(s["kn_ps"], 1)

            slot_ready(pe, 8)
            for i in range(NT):
                if i:
                    pe.wait_ge(s["conv_done"], CT)
                    k_pair(0)
                    k_pair(1)
                for b, lo, hi in ((0, 0, 512), (1, 512, HEADS * QKD)):
                    for f in range(QL // P):
                        last = mm(ps[:, 4 + 2 * i + b, 0:hi - lo], cqT[:, f, i * P:(i + 1) * P],
                                  ring[:, 0, f * HEADS * QKD + lo:f * HEADS * QKD + hi], f == 0, f == QL // P - 1)
                last.then_inc(s["q_ps"], 1)
            k_pair(2)
            k_pair(3)
            for i, m in enumerate((P, P, META)):
                pe.wait_ge(s["q_sb"], (1, 1, 2)[i])
                mm(ps[0:m, 4 + i, :], ckvT[:, i * P:i * P + m], wkv[:, HEADS * NOPE:HEADS * (NOPE + VD)], True, True
                   ).then_inc(s["v_ps"], 1)

            pe.wait_ge(s["kn_sb"], HEADS // 2)
            pe.wait_ge(s["kr_sb"], 1)
            pe.wait_ge(s["qr_done"], NT)
            for hp in range(HEADS // 2):
                for j in range(2):
                    for i in range(NT):
                        last = turn(ps[0:QKD, hp, j * TOK + i * P:j * TOK + (i + 1) * P],
                                    qtok[:, i, (2 * hp + j) * QKD:(2 * hp + j + 1) * QKD])
                        if hp == j == i == 0:
                            last.then_inc(used, Q_SLOT + 2)
                last.then_inc(s["qt_ps"], 1)

            pe.wait_ge(s["qt_act"], 2)
            pe.wait_ge(s["qt_dve"], 2)
            pe.wait_ge(s["v_sb"], 3)

            def scores(u):
                hd, i = u // 2, u % 2
                nk = META + P if i == 0 else COLS
                if u >= 3:
                    pe.wait_ge(s["s_sb"], u - 2)
                mm(ps[:, u % 3, 0:nk], qT[0:QKD, hd, i * P:(i + 1) * P], kT[0:QKD, hd, 0:nk], True, True
                   ).then_inc(s["s_ps"], 1)

            def key_tiles(i):
                return [(P, 0), (META, P)] if i == 0 else [(P, 0), (P, P), (META, 2 * P)]

            def turn_probs(u):
                pe.wait_ge(s["p_done"], u + 1)
                if u >= 2:
                    pe.wait_ge(s["pt_sb"], u - 1)
                for k, (m, c) in enumerate(key_tiles(u % 2)):
                    last = turn(ps[0:m, 3 + u % 2, k * P:(k + 1) * P], pm1[:, u % 3, c:c + m])
                last.then_inc(s["pt_ps"], 1)

            def values(u):
                hd, i = u // 2, u % 2
                pe.wait_ge(s["pt_sb"], u + 1)
                if hd >= 4 and u % 4 == 0:
                    pe.wait_ge(s["sq_done"], CT + hd // 2 - 1)
                o = ps[(hd % 2) * VD:(hd % 2 + 1) * VD, 6 + (hd // 2) % 2, i * P:(i + 1) * P]
                tiles = key_tiles(i)
                for k, (m, c) in enumerate(tiles):
                    last = mm(o, v1[0:m, k, hd * VD:(hd + 1) * VD], pt1[0:m, u % 2, k * P:(k + 1) * P],
                              k == 0, k == len(tiles) - 1)
                last.then_inc(s["o_ps"], 1)

            def conv_share(j, m):
                i, n = j // 2, j % 2
                split_ready(8 + m // 2, m % 2)
                if m == 0:
                    pe.wait_ge(s["convg_done"], CT)
                    if j:
                        pe.wait_ge(s["cm_sb"], j)
                c = (m % 2) * D + n * 512
                begin, last = triple(ps[:, 5, :], [x[:, CT + m, i * P:(i + 1) * P] for x in (mrg_hi, mrg_lo)],
                                     [w[m // 2][:, c:c + 512] for w in (w_hi, w_lo)], m == 0, m == CT - 1)
                if m == CT - 1:
                    last.then_inc(s["cm_ps"], 1)

            scores(0)
            scores(1)
            for u in range(2 * HEADS):
                if u + 2 < 2 * HEADS:
                    scores(u + 2)
                f = u - FILL
                if 0 <= f < 4 * NT:
                    conv_share(f // 2, 2 * (f % 2))
                    conv_share(f // 2, 2 * (f % 2) + 1)
                elif f == 4 * NT:
                    pe.wait_ge(s["cm_sb"], 2 * NT)
                    pe.wait_ge(s["sqs_done"], CT - 1)
                    for i in range(NT):
                        last = mm(ps[:, 5, 2 * i + 1:2 * i + 2], sq[:, CT, i * P:(i + 1) * P], ones[:, 0:1], True, True)
                        if i == 0:
                            last.then_inc(split_used, 2)
                turn_probs(u)
                if u:
                    values(u - 1)

            def mix_share(m):
                split_ready(10 + m // 2, m % 2)
                pe.wait_ge(s["att_low"], m + 1)
                for j in range(2 * NT):
                    i, n = j // 2, j % 2
                    c = (m % 2) * D + n * 512
                    begin, last = triple(ps[:, j, :], [x[:, m, i * P:(i + 1) * P] for x in (mrg_hi, mrg_lo)],
                                         [w[m // 2][:, c:c + 512] for w in (w_hi, w_lo)], m == 0, m == CT - 1)
                    if m == CT - 1:
                        last.then_inc(s["mix_ps"], 1)

            values(2 * HEADS - 1)
            for m in range(2):
                mix_share(m)
            pe.wait_ge(s["sq_done"], 2 * CT)
            pe.wait_ge(s["sqs_done"], 2 * CT - 3)
            for i in range(NT):
                mm(ps[:, 5, 2 * i:2 * i + 1], sq[:, 0, i * P:(i + 1) * P], ones[:, 0:1], True, False)
                last = mm(ps[:, 5, 2 * i:2 * i + 1], sq[:, CT - 1, i * P:(i + 1) * P], ones[:, 0:1], False, True)
            last.then_inc(s["ssm_ps"], 1)
            for m in range(2, CT):
                mix_share(m)

            pe.wait_ge(s["mix_done"], 2 * NT)
            pe.wait_ge(s["xn_done"], 1 + NT)
            for t in range(DT):
                for i in range(NT):
                    last = turn(ps[:, t, i * P:(i + 1) * P], xn1[:, i, t * P:(t + 1) * P])
                    if t == 0 and i == 0:
                        last.then_inc(split_used, 2)
                last.then_inc(s["turn_ps"], 1)

            pe.wait_ge(s["turn_act"], 8 + DT // 2)
            pe.wait_ge(s["turn_dve"], 8 + DT // 2)
            W = GROUPS + EXPERTS
            for t in range(DT):
                last = mm(ps[0:W, 7, 0:TOK], vec[:, V_ROUTE + t * W:V_ROUTE + (t + 1) * W], tT[:, t, :], t == 0, t == DT - 1)
                if t == 0:
                    last.then_inc(used, 4)
            last.then_inc(s["lt_ps"], 1)
            pe.wait_ge(s["lt_sb"], 1)
            for i in range(NT):
                last = turn(ps[:, 6, i * W:(i + 1) * W], logT[0:W, i * P:(i + 1) * P], W)
            last.then_inc(s["lg_ps"], 1)
            slot_ready(pe, 14)
            slot_ready(pe, 15)
            for f in range(2):
                if f:
                    pe.wait_ge(s["chosen_done"], 1)
                    E = EXPERTS
                    mm(ps[:, 7, 0:E], tri, chosen[:, 0, :], True, True)
                    mm(ps[:, 7, E:2 * E], ones, chosen[:, 0, :], True, False)
                    mm(ps[:, 7, E:2 * E], tri, chosen[:, 1, :], False, True)
                    mm(ps[:, 7, 2 * E:3 * E], ones, chosen[:, 0, :], True, False)
                    mm(ps[:, 7, 2 * E:3 * E], ones, chosen[:, 1, :], False, True).then_inc(s["rank_ps"], 1)
                for b in range(2):
                    for t in range(DT):
                        last = mm(ps[:, 4 + f, b * TOK:(b + 1) * TOK], ring[:, (14 + b) % SLOTS, t * FF + f * P:t * FF + (f + 1) * P],
                                  tT[:, t, :], t == 0, t == DT - 1)
                last.then_inc(s["sgu_ps"], 1)
            pe.wait_ge(s["hs_done"], 2)
            slot_ready(pe, 16)
            for i in range(NT):
                for n in range(2):
                    for f in range(2):
                        last = mm(ps[:, 2 * i + n, :], hs[:, f, i * P:(i + 1) * P],
                                  ring[:, 16 % SLOTS, f * D + n * 512:f * D + (n + 1) * 512], f == 0, False,
                                  skip_group_check=True)
                        if i == n == f == 0:
                            last.then_inc(used, 2)
            last.then_inc(used, 1)

            pe.wait_ge(s["xl_done"], NT)
            pe.wait_ge(s["rounds_done"], 1)
            rounds = pe.value_load(rounds_i[0:1, 0:1], min_val=1, max_val=GROUPS)
            with pe.Fori(0, rounds) as r:
                with pe.Fori(0, GROUPS) as g:
                    it = pe.snap(r * GROUPS + g)

                    def moe_slot(k):
                        n = B1 + k
                        pe.wait_ge(full[n % SLOTS], it * (16 * MOE_GROUP // SLOTS) + 16 * (n // SLOTS + 1))
                        return ring[:, n % SLOTS, :]

                    pe.wait_ge(s["sel_done"], it + 1)
                    for p in range(PAIRS):
                        for i in range(NT):
                            last = turn(ps[:, 4 + p // 2, (p % 2) * TOK + i * P:(p % 2) * TOK + (i + 1) * P],
                                        sel[:, i, p * P:(p + 1) * P].bitcast(F32))
                        if p % 2:
                            last.then_inc(s["st_ps"], 1)
                    for p in range(PAIRS):
                        for i in range(NT):
                            last = mm(ps[:, 6, 2 * p:2 * p + 2], sel[:, i, p * P:(p + 1) * P].bitcast(F32),
                                      comb[:, i, bass.ds(g * PER_GROUP + 2 * p, 2)], i == 0, i == NT - 1)
                    last.then_inc(s["st_ps"], 1)
                    for t in range(DT):
                        if 1 <= t < 4:
                            pe.wait_ge(s["st_sb"], it * 3 + t)
                        elif t >= 4 and t % 2 == 0:
                            pe.wait_ge(s["xg_act"], it * (DT // 2) + (t - 4) // 2 + 1)
                        elif t >= 4:
                            pe.wait_ge(s["xg_dve"], it * (DT // 2) + (t - 5) // 2 + 1)
                        for k, (a, i) in enumerate(((xh, 0), (xh, 1), (xl, 0), (xl, 1))):
                            last = mm(ps[:, gather_bank(t), :], a[:, i, t * P:(t + 1) * P], sel[:, i, :], k == 0, k == 3)
                        last.then_inc(s["xg_ps"], 1)
                    pe.wait_ge(s["xg_act"], it * (DT // 2) + DT // 2)
                    pe.wait_ge(s["xg_dve"], it * (DT // 2) + DT // 2)

                    def gate_up(p):
                        k0 = 4 * p if p < 2 else 6 * p - 2
                        for b in range(2):
                            w = [moe_slot(k0 + 2 * b), moe_slot(k0 + 2 * b + 1)]
                            for t in range(DT):
                                for e in range(2):
                                    last = mm(ps[e * CAP:(e + 1) * CAP, 4 + p % 2, b * FF:(b + 1) * FF],
                                              xg[:, t, (2 * p + e) * CAP:(2 * p + e + 1) * CAP],
                                              w[e][:, t * FF:(t + 1) * FF], t == 0, t == DT - 1)
                                    if t == e == 0 and b:
                                        last.then_inc(used, 2)
                        last.then_inc(s["gu_ps"], 1)

                    def turn_hidden(p):
                        pe.wait_ge(s["ht_done"], it * PAIRS + (p + 1))
                        for j in range(FF // P):
                            last = turn(ps[:, 4 + p % 2, j * P:(j + 1) * P], htok[:, j * P:(j + 1) * P])
                            if j == 0:
                                last.then_inc(used, 2)
                        last.then_inc(s["ht_ps"], 1)

                    def down(p, frees):
                        k0 = (8, 14, 20, 22)[p]
                        w = [moe_slot(k0), moe_slot(k0 + 1)]
                        pe.wait_ge(s["hid_done"], it * PAIRS + (p + 1))
                        for n in range(2):
                            for j in range(FF // P):
                                for e in range(2):
                                    last = mm(ps[e * CAP:(e + 1) * CAP, 6 + n, :], hid[:, j, e * CAP:(e + 1) * CAP],
                                              w[e][:, j * D + n * 512:j * D + (n + 1) * 512], j == 0, j == 1)
                                    if n == j == e == 0 and frees:
                                        last.then_inc(used, frees)
                            last.then_inc(s["y_ps"], 1)

                    def scatter(p, frees):
                        pe.wait_ge(s["yl_done"], it * (2 * PAIRS) + 2 * p + 2)
                        for q in range(2 * NT):
                            i, n = q // 2, q % 2
                            for k, y in enumerate((yh, yl)):
                                last = mm(ps[:, 2 * i + n, :], selT[:, p, i * P:(i + 1) * P], y[:, n * 512:(n + 1) * 512],
                                          False, False, skip_group_check=True)
                                if q == 0 and k == 0 and frees:
                                    last.then_inc(used, frees)
                        return last

                    for p in range(PAIRS):
                        gate_up(p)
                        if p >= 2:
                            scatter(p - 2, 2)
                        if p:
                            down(p - 1, 2 if p == 1 else 0)
                        turn_hidden(p)
                    scatter(PAIRS - 2, 0)
                    down(PAIRS - 1, 0)
                    scatter(PAIRS - 1, 2).then_inc(s["moe_done"], 1)

            pe.wait_ge(s["xn_done"], 3 + NT)
            for t in range(DT):
                for i in range(NT):
                    last = turn(ps[:, t, i * P:(i + 1) * P], xn2[:, i, t * P:(t + 1) * P])
                last.then_inc(s["turn_ps"], 1)
            for c in range(4):
                chunk(ps[:, c, 0:TOK], SPLIT1 + c // 2, c % 2, (u_hi, u_lo), frees=1 if c == 2 else 0,
                      turned_from=12 if c == 0 else None).then_inc(s["z2_ps"], 1)
            for c in range(CT):
                chunk(ps[:, 4 + c, 0:TOK], SPLIT1 + 2 + c // 2, c % 2, (u_hi, u_lo), frees=1 - c % 2).then_inc(s["q2_ps"], 1)
            for c in range(2):
                pe.wait_ge(s["z2_sb"], c + 1)
                chunk(ps[:, c, 0:TOK], SPLIT1 + 4, c, (u_hi, u_lo), frees=1 - c).then_inc(s["k2_ps"], 1)
            split_ready(SPLIT1 + 5, 0)
            pe.wait_ge(s["z2_sb"], 3)
            for i in range(NT):
                for t in range(DT):
                    begin, last = triple(ps[:, 2, i * P:(i + 1) * P], [u[:, t, i * P:(i + 1) * P] for u in (u_hi, u_lo)],
                                         [w[1][:, t * P:(t + 1) * P] for w in (w_hi, w_lo)], t == 0, t == DT - 1)
                    if t == i == 0:
                        begin.then_inc(split_used, 1)
            last.then_inc(s["v2_ps"], 1)
            pe.wait_ge(s["v2_sb"], 1)
            pe.wait_ge(s["q2_sb"], CT)
            pe.wait_ge(s["k2_sb"], 2)

            def scores2(u):
                hd, i = u // 2, u % 2
                lo = (hd % 2) * HD
                if u >= 2:
                    pe.wait_ge(s["s2_sb"], u - 1)
                mm(ps[:, 2 + u % 2, 0:TOK], q2T[lo:lo + HD, hd // 2, i * P:(i + 1) * P], k2T[lo:lo + HD, hd // 4, :],
                   True, True).then_inc(s["s2_ps"], 1)

            def turn_probs2(u):
                pe.wait_ge(s["p2_done"], u + 1)
                if u >= 2:
                    pe.wait_ge(s["pt2_sb"], u - 1)
                for k in range(NT):
                    last = turn(ps[:, 4 + u % 2, k * P:(k + 1) * P], pm2[:, u % 3, k * P:(k + 1) * P])
                last.then_inc(s["pt2_ps"], 1)

            def values2(u):
                hd, i = u // 2, u % 2
                kv = hd // 4
                pe.wait_ge(s["pt2_sb"], u + 1)
                if hd >= 4 and u % 4 == 0:
                    pe.wait_ge(s["o2_low"], hd // 2 - 1)
                o = ps[(hd % 2) * HD:(hd % 2 + 1) * HD, 6 + (hd // 2) % 2, i * P:(i + 1) * P]
                for k in range(NT):
                    last = mm(o, v2[:, k, kv * HD:(kv + 1) * HD], pt2[:, u % 2, k * P:(k + 1) * P], k == 0, k == NT - 1)
                last.then_inc(s["o2_ps"], 1)

            scores2(0)
            scores2(1)
            for u in range(2 * HEADS):
                m = u // 2
                if u % 2 == 0 and m >= 2:
                    pe.wait_ge(s["g_sb"], m - 1)
                last = chunk(ps[:, m % 2, (u % 2) * TOK:(u % 2 + 1) * TOK], SPLIT1 + 6 + m, u % 2, (u_hi, u_lo), frees=1 - u % 2)
                if u % 2:
                    last.then_inc(s["g_ps"], 1)
                if u + 2 < 2 * HEADS:
                    scores2(u + 2)
                turn_probs2(u)
                if u:
                    values2(u - 1)
            values2(2 * HEADS - 1)

            for c in range(4):
                pe.wait_ge(s["dp_done"], c + 1)
                if c == 2:
                    pe.wait_ge(s["g_sb"], DT)
                mm(ps[:, (4, 5, 0, 1)[c], 0:TOK], vec[:, V_PG + c * P:V_PG + (c + 1) * P], dp[:, c, :], True, True
                   ).then_inc(s["yp_ps"], 1)
            pe.wait_ge(s["yp_low"], 4)
            pe.wait_ge(s["o2_low"], CT)
            for m in range(DT):
                n = 14 + m // 2
                split_ready(SPLIT1 + n, m % 2)
                if m >= 4:
                    pe.wait_ge(s["br_sb"], m - 3)
                for b, src in ((0, (yp_hi, yp_lo)), (1, (at_hi, at_lo))):
                    for k in range(4):
                        c = (m % 2) * D + (4 * b + k) * P
                        begin, last = triple(ps[:, 2 + m % 4, b * TOK:(b + 1) * TOK],
                                             [w[n % 2][:, c:c + P] for w in (w_hi, w_lo)], [x[:, k, :] for x in src],
                                             k == 0, k == 3)
                        if m % 2 == b == k == 0:
                            begin.then_inc(split_used, 1)
                last.then_inc(s["br_ps"], 1)
            for k in range(DT):
                n = 18 + k // 2
                split_ready(SPLIT1 + n, k % 2)
                pe.wait_ge(s["mg_done"], k + 1)
                for q in range(2 * NT):
                    i, nn = q // 2, q % 2
                    c = (k % 2) * D + nn * 512
                    begin, last = triple(ps[:, (0, 1, 6, 7)[q], :], [x[:, k, i * P:(i + 1) * P] for x in (mg_hi, mg_lo)],
                                         [w[n % 2][:, c:c + 512] for w in (w_hi, w_lo)], k == 0, k == DT - 1)
                    if k % 2 == 0 and q == 0:
                        begin.then_inc(split_used, 1)
                    if k == DT - 1 and nn:
                        last.then_inc(s["h3_ps"], 1)

            pe.wait_ge(s["h3_done"], NT)
            pe.wait_ge(s["mg_done"], DT)
            pe.wait_ge(s["xn_done"], 5 + NT)
            for t in range(DT):
                for i in range(NT):
                    last = turn(ps[:, t, i * P:(i + 1) * P], xn2[:, i, t * P:(t + 1) * P])
                    if t == i == 0:
                        last.then_inc(split_used, 1)
                last.then_inc(s["turn_ps"], 1)

            def ffn_gate_up(m):
                n = ffn_slot(m)
                if m >= 4:
                    pe.wait_ge(s["fh_done"], m - 3)
                for b in range(2):
                    last = chunk(ps[:, 4 + m % 4, b * TOK:(b + 1) * TOK], SPLIT1 + n, b, (u_hi, u_lo),
                                 frees=1 if m and b == 0 else 0, turned_from=20 if m == b == 0 else None, bank=4)
                last.then_inc(s["f_ps"], 1)

            def ffn_down(i2):
                n = B2 + 4 + 3 * i2 if i2 < F2T // 2 - 1 else B2 + FFN_SLOTS - 1
                pair = (2 * i2, 2 * i2 + 1)
                steps = [(m, q) for m in pair for q in range(2 * NT)]
                if i2 == F2T // 2 - 1:
                    steps = [(m, 2 * i + nn) for i in range(NT) for m in pair for nn in range(2)]
                for k, (m, q) in enumerate(steps):
                    split_ready(SPLIT1 + n, m % 2)
                    pe.wait_ge(s["fh_done"], m + 1)
                    i, nn = q // 2, q % 2
                    c = (m % 2) * D + nn * 512
                    begin, last = triple(ps[:, q, :], [x[:, m % 4, i * P:(i + 1) * P] for x in (fh_hi, fh_lo)],
                                         [w[n % 2][:, c:c + 512] for w in (w_hi, w_lo)], m == 0, m == F2T - 1)
                    if k == 0:
                        begin.then_inc(split_used, 1)
                    if m == F2T - 1 and nn:
                        last.then_inc(s["facc_ps"], 1)

            ffn_gate_up(0)
            ffn_gate_up(1)
            for i2 in range(F2T // 2):
                if i2 < F2T // 2 - 1:
                    ffn_gate_up(2 * i2 + 2)
                    ffn_gate_up(2 * i2 + 3)
                ffn_down(i2)


def shape_constants():
    import numpy as np
    c = np.zeros((P, CN), np.float32)
    c[:, C_ID:C_ID + P] = np.eye(P)
    q = np.arange(P)[:, None]
    k = np.arange(P)[None, :]
    c[:, C_MASK + COLS - P:C_MASK + COLS] = np.where(k <= q, 0.0, -BIG)
    c[:, C_TRI:C_TRI + P] = q < k
    c[:, C_ONE:C_ONE + P] = 1.0
    c[:, C_IOTA:C_IOTA + CAP] = np.arange(CAP)
    c[:, C_DESC:C_DESC + EXPERTS] = EXPERTS - np.arange(EXPERTS)
    for i in range(NT):
        dist = np.abs(q + i * P - np.arange(TOK)[None, :]).astype(np.float32)
        c[:, C_DIST + i * TOK:C_DIST + (i + 1) * TOK] = np.where(dist <= 128, dist, 1e34)
    t = np.arange(TOK)
    for g, w in enumerate(POOL_WINDOWS):
        n = np.clip(t + w // 2, 0, TOK) - np.clip(t - w // 2, 0, TOK)
        c[:, C_CNT + g * TOK:C_CNT + (g + 1) * TOK] = 1.0 / n
    f = np.float32(1.0) / (np.float32(10000.0) ** (np.arange(0, ROPE, 2, dtype=np.float32) / np.float32(ROPE)))
    c[:, C_FREQ:C_FREQ + ROPE // 2] = f
    c[0:META, C_POS] = np.arange(META)
    c[:, C_NHALF] = -0.5
    return c


def packed(inputs):
    import numpy as np

    def per_partition(name, i0=0):
        a = np.asarray(inputs[name])[i0].reshape(-1, P)
        return a.T

    def over(a):
        return np.broadcast_to(np.asarray(a).reshape(1, -1), (P, np.asarray(a).size))

    conv = np.asarray(inputs["conv_w"])[0].reshape(3 * CT, P).T
    route = np.concatenate([np.asarray(inputs["w_group_router"])[0], np.asarray(inputs["w_expert_router"])[0]], 1)
    route = route.reshape(DT, P, -1).transpose(1, 0, 2).reshape(P, -1)
    maps = np.asarray(inputs["w_pool_group_2"])[0].transpose(1, 0, 2).reshape(P, -1)
    small = np.concatenate([
        per_partition("pre_mix_norm"), per_partition("q_norm"), per_partition("kv_norm"), conv,
        per_partition("attn_out_norm"), per_partition("conv_out_norm"), per_partition("pre_ffn_norm"),
        per_partition("norm_mix_2"), per_partition("norm_ffn_2"), per_partition("pool_scale_2"),
        over(inputs["b_group_router"]), over(inputs["b_expert_router"]), over(inputs["sink_2"]), route, maps], 1)
    assert small.shape == (P, VN)
    gains = np.stack([over(inputs[n]) for n in ("post_mix_norm", "post_ffn_norm", "norm_final_2")], 1)
    return np.ascontiguousarray(small), np.ascontiguousarray(gains)


def weight_stream(inputs):
    import numpy as np
    w = {k: np.asarray(inputs[k])[0] for k in (
        "w_in", "w_uq", "w_ukv", "w_out", "w_sh_gate", "w_sh_up", "w_sh_down", "w_gate", "w_up", "w_down", "w_in_2",
        "w_pool_branch_2", "w_attn_branch_2", "w_out_2", "w_ffn_gate_2", "w_ffn_up_2", "w_ffn_down_2")}
    out = np.zeros((STREAM, P, SLOT), np.float32)
    at = [0]

    def put(*parts):
        c = 0
        for a in parts:
            a = a.reshape(a.shape[0] // P, P, a.shape[1]).transpose(1, 0, 2).reshape(P, -1)
            out[at[0], :, c:c + a.shape[1]] = a
            c += a.shape[1]
        at[0] += 1

    def cols(a, lo, n=P):
        return a[:, lo:lo + n]

    wi = w["w_in"]
    put(wi[0:D // 2, 0:ZA])
    put(wi[D // 2:D, 0:ZA])
    gb, gc, xi = ZA, ZA + 512, ZA + 1024
    chunks = [cols(wi, base + m * P) for m in range(CT) for base in (gc, xi, gb)]
    for c in range(0, len(chunks), 2):
        put(chunks[c], chunks[c + 1])
    put(w["w_uq"])
    kv = w["w_ukv"].reshape(KVL, HEADS, NOPE + VD)
    put(kv[:, :, 0:NOPE].reshape(KVL, -1), kv[:, :, NOPE:].reshape(KVL, -1))
    for k in (2, 3, 0, 1):
        put(w["w_out"][k * 256:(k + 1) * 256])
    put(w["w_sh_gate"])
    put(w["w_sh_up"])
    put(w["w_sh_down"])
    for e in range(0, EXPERTS, 2):
        pair = (e // 2) % PAIRS
        for name in ("w_gate", "w_up"):
            put(w[name][e])
            put(w[name][e + 1])
        for back in ((), (2,), (2,), (2, 0))[pair]:
            put(w["w_down"][e - back])
            put(w["w_down"][e - back + 1])
    w2 = w["w_in_2"]
    q0, k0, v0, gp0, ga0 = 512, 1024, 1152, 1280, 2304
    for c in range(0, 4, 2):
        put(cols(w2, c * P), cols(w2, (c + 1) * P))
    for c in range(0, 4, 2):
        put(cols(w2, q0 + c * P), cols(w2, q0 + (c + 1) * P))
    ka, kb = cols(w2, k0, HD), cols(w2, k0 + HD, HD)
    put(np.concatenate([ka, ka], 1), np.concatenate([kb, kb], 1))
    put(cols(w2, v0))
    for m in range(DT):
        put(cols(w2, gp0 + m * P), cols(w2, ga0 + m * P))
    branches = [cols(w[name], m * P) for m in range(DT) for name in ("w_pool_branch_2", "w_attn_branch_2")]
    for m in range(0, 2 * DT, 4):
        put(*branches[m:m + 4])
    for k in range(4):
        put(w["w_out_2"][k * 256:(k + 1) * 256])
    gate, up, down = w["w_ffn_gate_2"], w["w_ffn_up_2"], w["w_ffn_down_2"]
    for m in (0, 1):
        put(cols(gate, m * P), cols(up, m * P))
    for i in range(F2T // 2):
        if i < F2T // 2 - 1:
            for m in (2 * i + 2, 2 * i + 3):
                put(cols(gate, m * P), cols(up, m * P))
        put(down[i * 256:(i + 1) * 256])
    assert at[0] == STREAM, (at[0], STREAM)
    return out


def kernel(**inputs):
    import numpy as np
    import concourse.bacc as bacc
    from concourse.bass_utils import run_bass_kernel_spmd

    small, gains = packed(inputs)
    arrays = {
        "x": np.ascontiguousarray(np.asarray(inputs["x"])[0]),
        "meta": np.ascontiguousarray(np.asarray(inputs["meta_tokens"])),
        "consts": shape_constants(),
        "small": small,
        "gains": gains,
        "positions": np.ascontiguousarray(np.asarray(inputs["positions"])[0].reshape(NT, P).T),
        "stream": weight_stream(inputs),
    }
    nc = bacc.Bacc("TRN2", target_bir_lowering=False, num_devices=1)
    args = [nc.dram_tensor(f"{n}_dram", a.shape, mybir.dt.from_np(a.dtype), kind="ExternalInput").ap()
            for n, a in arrays.items()]
    out = nc.dram_tensor("out_dram", (TOK, D), F32, kind="ExternalOutput").ap()
    two_blocks(nc, *args, out)
    r = run_bass_kernel_spmd(nc, [{f"{n}_dram": a for n, a in arrays.items()}], core_ids=[0])
    return r.results[0]["out_dram"].reshape(1, TOK, D)
```
